# Optimizing a Trainium2 kernel written in Bass

```python
import math
import jax, jax.numpy as jnp
from jax import lax
import numpy as np

D_MODEL = 1024
BATCH = 1
SEQ = 512
DEPTH = 1
DEC_BATCH = 8
DEC_SEQ = 1
PAST_LEN = 4096
PAGE_SIZE = 128

N_META = 16
D_MIX = 2 * D_MODEL
SSD_WIDTH = D_MODEL // 1
SSD_HEAD_DIM = 64
SSD_HEADS = SSD_WIDTH // SSD_HEAD_DIM
SSD_GROUPS = 2
SSD_HPG = SSD_HEADS // SSD_GROUPS
SSD_STATE = 128
SSD_CONV = 4
SSD_CHUNK = 128
SSD_CONV_DIM = SSD_WIDTH + 2 * SSD_GROUPS * SSD_STATE
S5_WIDTH = D_MIX - SSD_WIDTH
S5_GROUP_CH = 16
S5_GROUPS = S5_WIDTH // S5_GROUP_CH
S5_STATE = 64
IN_COLS = SSD_WIDTH + SSD_CONV_DIM + SSD_HEADS + S5_WIDTH
MOE_GROUPS = 4
MOE_EPG = 8
MOE_EXPERTS = MOE_GROUPS * MOE_EPG
MOE_TOP_K = 2
MOE_D_FF = 512
EPS = 1e-6

kernel_name = 'hymba_ssd_s5_hiermoe_step'

def _rmsnorm(x, g):
    xf = x.astype(jnp.float32)
    y = xf * lax.rsqrt(jnp.mean(xf * xf, axis=-1, keepdims=True) + EPS)
    return y.astype(x.dtype) * g

def _causal_conv(xbc, prefix, w, b):
    L = xbc.shape[1]
    xp = jnp.concatenate([prefix.astype(xbc.dtype), xbc], axis=1)
    out = b
    for k in range(SSD_CONV):
        out = out + xp[:, k:k + L] * w[k]
    return jax.nn.silu(out), xp[:, L:]

def _ssd_chunked(x, dt, A, B, C, D, h0, chunk):
    bsz, L = x.shape[0], x.shape[1]
    nc = L // chunk
    xc = x.reshape(bsz, nc, chunk, SSD_GROUPS, SSD_HPG, SSD_HEAD_DIM)
    dtc = dt.reshape(bsz, nc, chunk, SSD_GROUPS, SSD_HPG)
    Bc = B.reshape(bsz, nc, chunk, SSD_GROUPS, SSD_STATE)
    Cc = C.reshape(bsz, nc, chunk, SSD_GROUPS, SSD_STATE)
    Ag = A.reshape(SSD_GROUPS, SSD_HPG)
    dA = (dtc * Ag).astype(jnp.float32)
    cs = jnp.cumsum(dA, axis=2)
    seg = cs[:, :, :, None] - cs[:, :, None, :]
    mask = jnp.tril(jnp.ones((chunk, chunk), dtype=bool))[:, :, None, None]
    Lmat = jnp.exp(jnp.where(mask, seg, -jnp.inf))
    cb = jnp.einsum('bclgn,bcsgn->bclsg', Cc, Bc)
    M = cb[..., None] * Lmat * dtc[:, :, None]
    y_diag = jnp.einsum('bclsgk,bcsgkp->bclgkp', M, xc)
    decay_end = jnp.exp(cs[:, :, -1:] - cs)
    states = jnp.einsum('bclgn,bclgk,bclgkp->bcgkpn', Bc, decay_end * dtc, xc).astype(jnp.float32)
    chunk_decay = jnp.exp(cs[:, :, -1])

    def step(h, inp):
        s, d = inp
        return d[..., None, None] * h + s, h

    h_init = h0.reshape(bsz, SSD_GROUPS, SSD_HPG, SSD_HEAD_DIM, SSD_STATE).astype(jnp.float32)
    h_last, h_prev = lax.scan(step, h_init, (jnp.moveaxis(states, 1, 0), jnp.moveaxis(chunk_decay, 1, 0)))
    h_prev = jnp.moveaxis(h_prev, 0, 1)
    y_off = jnp.einsum('bclgn,bcgkpn,bclgk->bclgkp', Cc, h_prev, jnp.exp(cs))
    y = y_diag + y_off + D.reshape(SSD_GROUPS, SSD_HPG)[..., None] * xc
    y = y.reshape(bsz, L, SSD_HEADS, SSD_HEAD_DIM).astype(x.dtype)
    return y, h_last.reshape(bsz, SSD_HEADS, SSD_HEAD_DIM, SSD_STATE).astype(x.dtype)

def _s5_combine(e1, e2):
    a1r, a1i, b1r, b1i = e1
    a2r, a2i, b2r, b2i = e2
    ar = a1r * a2r - a1i * a2i
    ai = a1r * a2i + a1i * a2r
    br = a2r * b1r - a2i * b1i + b2r
    bi = a2r * b1i + a2i * b1r + b2i
    return (ar, ai, br, bi)

def _s5_group(u, h0_re, h0_im, a_re, a_im, log_dt, b_re, b_im, c_re, c_im, d, w_glu, b_glu, gain):
    bsz, L = u.shape[0], u.shape[1]
    ug = u.reshape(bsz, L, S5_GROUPS, S5_GROUP_CH).transpose(1, 0, 2, 3)
    dt = jnp.exp(log_dt)[:, None]
    mag = jnp.exp(a_re * dt)
    ab_re = mag * jnp.cos(a_im * dt)
    ab_im = mag * jnp.sin(a_im * dt)
    den = a_re * a_re + a_im * a_im
    nr = ab_re - 1.0
    q_re = (nr * a_re + ab_im * a_im) / den
    q_im = (ab_im * a_re - nr * a_im) / den
    bb_re = q_re[..., None] * b_re - q_im[..., None] * b_im
    bb_im = q_re[..., None] * b_im + q_im[..., None] * b_re
    bu_re = jnp.einsum('lbgc,gpc->lbgp', ug, bb_re)
    bu_im = jnp.einsum('lbgc,gpc->lbgp', ug, bb_im)
    a_seq_re = jnp.broadcast_to(ab_re[None, None], (L, 1, S5_GROUPS, S5_STATE))
    a_seq_im = jnp.broadcast_to(ab_im[None, None], (L, 1, S5_GROUPS, S5_STATE))
    acr, aci, hr, hi = lax.associative_scan(_s5_combine, (a_seq_re, a_seq_im, bu_re, bu_im), axis=0)
    hr = hr + acr * h0_re[None] - aci * h0_im[None]
    hi = hi + acr * h0_im[None] + aci * h0_re[None]
    y = jnp.einsum('lbgp,gcp->lbgc', hr, c_re) - jnp.einsum('lbgp,gcp->lbgc', hi, c_im) + d * ug
    y = y.transpose(1, 0, 2, 3).reshape(bsz, L, S5_WIDTH)
    y = jax.nn.gelu(y)
    y = y * jax.nn.sigmoid(y @ w_glu + b_glu)
    return _rmsnorm(y, gain), hr[-1], hi[-1]

def _hier_moe(x, rc_w, rc_b, rf_w, rf_b, w_gate, w_up, w_down):
    bsz, L, dm = x.shape
    t = x.reshape(-1, dm)
    lc = (t @ rc_w + rc_b).astype(jnp.float32)
    pc = jax.nn.softmax(lc, axis=-1)
    g_sel = jnp.argmax(lc, axis=-1)
    p_sel = jnp.take_along_axis(pc, g_sel[:, None], axis=-1)
    lf = jnp.einsum('td,gde->tge', t, rf_w) + rf_b
    lf_sel = jnp.take_along_axis(lf, g_sel[:, None, None], axis=1)[:, 0].astype(jnp.float32)
    pf = jax.nn.softmax(lf_sel, axis=-1)
    vals, idx = lax.top_k(pf, MOE_TOP_K)
    vals = vals / jnp.sum(vals, axis=-1, keepdims=True)
    eid = g_sel[:, None] * MOE_EPG + idx
    gates = p_sel * jnp.einsum('tk,tke->te', vals, jax.nn.one_hot(eid, MOE_EXPERTS, dtype=jnp.float32))
    gates = gates.astype(t.dtype)
    out = jnp.zeros_like(t)
    for e in range(MOE_EXPERTS):
        h = jax.nn.silu(t @ w_gate[e]) * (t @ w_up[e])
        out = out + gates[:, e:e + 1] * (h @ w_down[e])
    return out.reshape(bsz, L, dm)

def _layer(x, conv_prefix, ssm_h0, s5_h0_re, s5_h0_im, pad_front, chunk,
           norm_mix, w_in, conv_w, conv_b, dt_bias, a_log, d_ssd, ssd_norm,
           s5_a_re, s5_a_im, s5_log_dt, s5_b_re, s5_b_im, s5_c_re, s5_c_im, s5_d,
           w_glu, b_glu, s5_norm, w_out, norm_ffn, rc_w, rc_b, rf_w, rf_b,
           w_gate, w_up, w_down):
    bsz, L, _ = x.shape
    xn = _rmsnorm(x, norm_mix)
    proj = xn @ w_in
    z, xbc, dt_raw, u = jnp.split(
        proj, [SSD_WIDTH, SSD_WIDTH + SSD_CONV_DIM, SSD_WIDTH + SSD_CONV_DIM + SSD_HEADS], axis=-1)
    xbc, new_conv = _causal_conv(xbc, conv_prefix, conv_w, conv_b)
    xs, bm, cm = jnp.split(xbc, [SSD_WIDTH, SSD_WIDTH + SSD_GROUPS * SSD_STATE], axis=-1)
    dt = jax.nn.softplus(dt_raw + dt_bias)
    xs = xs.reshape(bsz, L, SSD_HEADS, SSD_HEAD_DIM)
    bm = bm.reshape(bsz, L, SSD_GROUPS, SSD_STATE)
    cm = cm.reshape(bsz, L, SSD_GROUPS, SSD_STATE)
    if pad_front > 0:
        padf = lambda a: jnp.pad(a, [(0, 0), (pad_front, 0)] + [(0, 0)] * (a.ndim - 2))
        xs, dt, bm, cm = padf(xs), padf(dt), padf(bm), padf(cm)
    y, new_ssm = _ssd_chunked(xs, dt, -jnp.exp(a_log), bm, cm, d_ssd, ssm_h0, chunk)
    y = y[:, pad_front:].reshape(bsz, L, SSD_WIDTH)
    y_ssd = _rmsnorm(y * jax.nn.silu(z), ssd_norm)
    y_s5, new_re, new_im = _s5_group(u, s5_h0_re, s5_h0_im, s5_a_re, s5_a_im, s5_log_dt,
                                     s5_b_re, s5_b_im, s5_c_re, s5_c_im, s5_d, w_glu, b_glu, s5_norm)
    x = x + jnp.concatenate([y_ssd, y_s5], axis=-1) @ w_out
    x = x + _hier_moe(_rmsnorm(x, norm_ffn), rc_w, rc_b, rf_w, rf_b, w_gate, w_up, w_down)
    return x, new_conv, new_ssm, new_re, new_im

def setup_inputs(seed: int = 0) -> dict:
    key = jax.random.key(seed)
    ks = iter(jax.random.split(key, 48))
    f32 = jnp.float32
    nrm = lambda shape, scale: jax.random.normal(next(ks), shape, f32) * scale
    P_ = DEPTH
    dt0 = jnp.exp(jax.random.uniform(next(ks), (P_, SSD_HEADS), f32, math.log(1e-3), math.log(1e-1)))
    dt_bias = dt0 + jnp.log(-jnp.expm1(-dt0))
    a_log = jnp.log(jax.random.uniform(next(ks), (P_, SSD_HEADS), f32, 1.0, 16.0))
    s5_a_re = -0.5 + nrm((P_, S5_GROUPS, S5_STATE), 0.01)
    s5_a_im = math.pi * jnp.arange(S5_STATE, dtype=f32)[None, None] + nrm((P_, S5_GROUPS, S5_STATE), 0.01)
    s5_log_dt = jax.random.uniform(next(ks), (P_, S5_GROUPS), f32, math.log(1e-3), math.log(1e-1))
    return {
        'x_prompt': nrm((BATCH, SEQ, D_MODEL), 1.0),
        'x_sample': nrm((DEC_BATCH, DEC_SEQ, D_MODEL), 1.0),
        'state_ssd_conv': nrm((DEPTH, DEC_BATCH, SSD_CONV - 1, SSD_CONV_DIM), 1.0),
        'state_ssd_ssm': nrm((DEPTH, DEC_BATCH, SSD_HEADS, SSD_HEAD_DIM, SSD_STATE), 0.5),
        'state_s5_re': nrm((DEPTH, DEC_BATCH, S5_GROUPS, S5_STATE), 1.0),
        'state_s5_im': nrm((DEPTH, DEC_BATCH, S5_GROUPS, S5_STATE), 1.0),
        'meta_tokens': nrm((N_META, D_MODEL), 1.0),
        'norm_mix': 1.0 + nrm((P_, D_MODEL), 0.02),
        'w_in': nrm((P_, D_MODEL, IN_COLS), D_MODEL ** -0.5),
        'conv_w': nrm((P_, SSD_CONV, SSD_CONV_DIM), 0.5),
        'conv_b': nrm((P_, SSD_CONV_DIM), 0.01),
        'dt_bias': dt_bias,
        'a_log': a_log,
        'd_ssd': 1.0 + nrm((P_, SSD_HEADS), 0.02),
        'ssd_norm': 1.0 + nrm((P_, SSD_WIDTH), 0.02),
        's5_a_re': s5_a_re,
        's5_a_im': s5_a_im,
        's5_log_dt': s5_log_dt,
        's5_b_re': nrm((P_, S5_GROUPS, S5_STATE, S5_GROUP_CH), (2 * S5_GROUP_CH) ** -0.5),
        's5_b_im': nrm((P_, S5_GROUPS, S5_STATE, S5_GROUP_CH), (2 * S5_GROUP_CH) ** -0.5),
        's5_c_re': nrm((P_, S5_GROUPS, S5_GROUP_CH, S5_STATE), (2 * S5_STATE) ** -0.5),
        's5_c_im': nrm((P_, S5_GROUPS, S5_GROUP_CH, S5_STATE), (2 * S5_STATE) ** -0.5),
        's5_d': nrm((P_, S5_GROUPS, S5_GROUP_CH), 0.5),
        'w_glu': nrm((P_, S5_WIDTH, S5_WIDTH), S5_WIDTH ** -0.5),
        'b_glu': nrm((P_, S5_WIDTH), 0.01),
        's5_norm': 1.0 + nrm((P_, S5_WIDTH), 0.02),
        'w_out': nrm((P_, D_MIX, D_MODEL), D_MIX ** -0.5),
        'norm_ffn': 1.0 + nrm((P_, D_MODEL), 0.02),
        'router_coarse_w': nrm((P_, D_MODEL, MOE_GROUPS), D_MODEL ** -0.5),
        'router_coarse_b': nrm((P_, MOE_GROUPS), 0.01),
        'router_fine_w': nrm((P_, MOE_GROUPS, D_MODEL, MOE_EPG), D_MODEL ** -0.5),
        'router_fine_b': nrm((P_, MOE_GROUPS, MOE_EPG), 0.01),
        'w_gate': nrm((P_, MOE_EXPERTS, D_MODEL, MOE_D_FF), D_MODEL ** -0.5),
        'w_up': nrm((P_, MOE_EXPERTS, D_MODEL, MOE_D_FF), D_MODEL ** -0.5),
        'w_down': nrm((P_, MOE_EXPERTS, MOE_D_FF, D_MODEL), MOE_D_FF ** -0.5),
        'norm_final': 1.0 + nrm((D_MODEL,), 0.02),
    }

def reference(x_prompt, x_sample, state_ssd_conv, state_ssd_ssm, state_s5_re, state_s5_im,
              meta_tokens, norm_mix, w_in, conv_w, conv_b, dt_bias, a_log, d_ssd, ssd_norm,
              s5_a_re, s5_a_im, s5_log_dt, s5_b_re, s5_b_im, s5_c_re, s5_c_im, s5_d,
              w_glu, b_glu, s5_norm, w_out, norm_ffn, router_coarse_w, router_coarse_b,
              router_fine_w, router_fine_b, w_gate, w_up, w_down, norm_final):
    bp = x_prompt.shape[0]
    meta = jnp.broadcast_to(meta_tokens.astype(x_prompt.dtype)[None], (bp, N_META, D_MODEL))
    xp = jnp.concatenate([meta, x_prompt], axis=1)
    pad_front = (-xp.shape[1]) % SSD_CHUNK
    xs = x_sample
    bs = xs.shape[0]
    conv_p, ssm_p, re_p, im_p = [], [], [], []
    conv_s, ssm_s, re_s, im_s = [], [], [], []
    for l in range(DEPTH):
        lp = (norm_mix[l], w_in[l], conv_w[l], conv_b[l], dt_bias[l], a_log[l], d_ssd[l], ssd_norm[l],
              s5_a_re[l], s5_a_im[l], s5_log_dt[l], s5_b_re[l], s5_b_im[l], s5_c_re[l], s5_c_im[l], s5_d[l],
              w_glu[l], b_glu[l], s5_norm[l], w_out[l], norm_ffn[l], router_coarse_w[l], router_coarse_b[l],
              router_fine_w[l], router_fine_b[l], w_gate[l], w_up[l], w_down[l])
        xp, c1, h1, r1, i1 = _layer(
            xp,
            jnp.zeros((bp, SSD_CONV - 1, SSD_CONV_DIM), xp.dtype),
            jnp.zeros((bp, SSD_HEADS, SSD_HEAD_DIM, SSD_STATE), xp.dtype),
            jnp.zeros((bp, S5_GROUPS, S5_STATE), xp.dtype),
            jnp.zeros((bp, S5_GROUPS, S5_STATE), xp.dtype),
            pad_front, SSD_CHUNK, *lp)
        xs, c2, h2, r2, i2 = _layer(
            xs, state_ssd_conv[l], state_ssd_ssm[l], state_s5_re[l], state_s5_im[l],
            0, xs.shape[1], *lp)
        conv_p.append(c1); ssm_p.append(h1); re_p.append(r1); im_p.append(i1)
        conv_s.append(c2); ssm_s.append(h2); re_s.append(r2); im_s.append(i2)
    y_prompt = _rmsnorm(xp, norm_final)[:, N_META:]
    y_sample = _rmsnorm(xs, norm_final)
    new_conv_prompt = jnp.stack(conv_p, 0)
    new_ssm_prompt = jnp.stack(ssm_p, 0)
    new_s5_re_prompt = jnp.stack(re_p, 0)
    new_s5_im_prompt = jnp.stack(im_p, 0)
    new_conv_sample = jnp.stack(conv_s, 0)
    new_ssm_sample = jnp.stack(ssm_s, 0)
    new_s5_re_sample = jnp.stack(re_s, 0)
    new_s5_im_sample = jnp.stack(im_s, 0)
    return (y_prompt, y_sample, new_conv_prompt, new_ssm_prompt, new_s5_re_prompt, new_s5_im_prompt,
            new_conv_sample, new_ssm_sample, new_s5_re_sample, new_s5_im_sample)


_drawn_inputs = setup_inputs


def setup_inputs(seed=0):
    import zlib

    import numpy as np

    out = dict(_drawn_inputs(seed))
    spreads = {}
    factors = {'conv_b': 2.889,
     'd_ssd': 3.513,
     'ssd_norm': 3.206,
     's5_a_re': 4.23,
     'b_glu': 5.81,
     's5_norm': 2.707,
     'norm_ffn': 3.101,
     'router_coarse_b': 5.521,
     'router_fine_b': 3.941,
     'norm_final': 2.941}
    for name, (base, spread) in spreads.items():
        noise = np.random.default_rng([zlib.crc32(name.encode()), seed]).standard_normal(out[name].shape)
        drawn = base * np.exp(spread * noise) if base else spread * noise
        out[name] = __import__('jax').numpy.asarray(drawn.astype(out[name].dtype))
    for name, factor in factors.items():
        out[name] = (out[name] * factor).astype(out[name].dtype)
    return out
```

```python
from contextlib import ExitStack

import numpy as np
import concourse.bass as bass
from concourse import mybir

F32 = mybir.dt.float32
BF16 = mybir.dt.bfloat16
I32 = mybir.dt.int32
ACT = mybir.ActivationFunctionType
ALU = mybir.AluOpType
AX = mybir.AxisListType

P = 128
D = 1024
KD = D // P
SEQ = 512
META = 16
NP_ = META + SEQ
NS = 8
N = NP_ + NS
SPLIT = 264
HALVES = ((0, SPLIT), (SPLIT, N))
TT = [(i * P, min(P, N - i * P)) for i in range(5)]
CH = [(i * P, min(P, NP_ - i * P)) for i in range(5)]
EPS = 1e-6

HEADS, HD, NSTATE, CONV = 16, 64, 128, 4
XBC = 12

G5, C5, S5 = 64, 16, 64
J = 8
NC5 = NP_ // J
COL_S0 = NC5 + 1
COL_S7 = COL_S0 + NS
UC = COL_S7 + NS
WIN = 96
YC = COL_S7

E, EPG, EG, FF = 32, 8, 4, 512
T = 64
MAXT = E + (2 * N) // (T + 1)
IDXC = 56
RING = 4

PF_GMIX, PF_CW, PF_CB, PF_D, PF_GSSD, PF_GS5, PF_BGLU, PF_ALOG, PF_N = 0, 8, 56, 68, 76, 84, 92, 100, 108
C_ID, C_TRI, C_SGN, C_M0, C_M1, C_IO8, C_IO4, C_VAL, C_N = 0, 128, 256, 257, 258, 259, 267, 271, 276

MAGIC = 12582912.0
TWO_PI_HI, TWO_PI_MID = 6.28125, 0.0019340515136718750
TWO_PI_LO = 2 * np.pi - TWO_PI_HI - TWO_PI_MID
PI_F = 3.1415925


def build(nc, a):
    ctx = ExitStack()
    with ctx:
        def sb(name, shape, dt=F32):
            return ctx.enter_context(nc.sbuf_tensor("sb_" + name, shape, dt))

        def sem(name):
            return ctx.enter_context(nc.semaphore(name))

        def scratch(name, shape, dt=F32):
            return nc.dram_tensor(name, shape, dt, kind="Internal").ap()

        u_scr = scratch("u_scr", [D, N])
        q_scr = scratch("q_scr", [J, G5 * 2 * S5])
        y_scr = scratch("y_scr", [D, N])
        x2_scr = scratch("x2_scr", [N, D])
        tok_scr = scratch("tok_scr", [IDXC * T, 1], I32)
        ye_scr = scratch("ye_scr", [MAXT * T, D])

        arena = sb("arena", [P, 47408])

        def part(off, *shape, p=(0, P)):
            n = int(np.prod(shape))
            v = arena[p[0]:p[1], off:off + n]
            if len(shape) == 1:
                return v
            names = "abcd"[:len(shape)]
            return v.rearrange(f"p ({' '.join(names)}) -> p {' '.join(names)}",
                               **{k: s for k, s in zip(names, shape)})

        xn = part(0, KD, N)
        ring = [part(4288 + 1024 * i, KD, P) for i in range(3)]
        raw = [part(7360 + 576 * i, 576) for i in range(2)]
        xcB = part(8512, 4, N)
        xcX = part(10656, 8, N)
        uD = [part(10656 + N * i, N) for i in range(2)]
        Vm = part(10656, 32, 2, S5)
        dt_raw = part(34864, N, p=(0, HEADS))
        sp_u, sp_s, sp_z = (part(35400 + 80 * i, 80) for i in range(3))
        wdt = part(14752, KD, HEADS)
        U = part(14944, 5328)
        Wp = part(20272, G5, J + 1, C5)
        HA_off = 29488
        xT = part(29488, KD, N)
        sq0 = part(33776, KD, N)
        Wt = part(29488, G5, J + 1, C5)
        rms0 = part(20272, N)
        pw_t = part(33776, 4 * G5)
        smp = part(34352, NS, G5)
        dkt = part(38704, 16, C5)
        stk = part(39216, 4, G5, C5)
        QB = part(39216, 32, 2, S5)
        BT = part(43312, 32, 2, S5)
        Tm = part(39216, G5, J, C5)
        Bb = part(39216 + 2048, (G5 + 1) * C5)
        tmp = 43312

        def tv(i):
            return part(tmp + G5 * i, G5)

        Pre, Pim = part(tmp + 1280, J + 1, G5), part(tmp + 1856, J + 1, G5)
        Qs, qt = part(tmp + 2432, J, G5), part(tmp + 2944, 4, P)
        zT = part(35632, 8, N)
        Lm = part(39920, HEADS, P)
        E2 = part(41968, HEADS, P)
        xdt = part(44016, HEADS, HD)
        xde = part(45040, HEADS, HD)
        cbm = part(46064, 2, P)
        btok = part(46320, 2, P)
        ySSD = xcX
        bts = part(20352, 4, NSTATE)
        h0b = [part(20864 + 1024 * i, 8, NSTATE) for i in range(2)]
        smt, smu, smv = (part(22912 + 1024 * i, 8, NSTATE) for i in range(3))
        bcb = [part(25984 + 512 * i, 4, NSTATE) for i in range(NS)]
        yraw = part(14944, 8, N)
        yg = part(0, KD, N)
        sig = part(30832, KD, N)
        sq = part(39920, KD, N)
        wo = [part(14944, KD, 512), part(4288, KD, 512)]
        x1 = [part(o, D) for o in (0, 1024, 2048, 3072, 19040)]
        W_off = [35120, 22640]
        Wg = [part(o, KD, FF) for o in W_off]
        Wu = [part(o + 4096, KD, FF) for o in W_off]
        Wd = [part(o + 8192, 4, D) for o in W_off]
        xg = [part(4288 + 1024 * i, D, p=(0, T)) for i in range(RING)]
        gffn = part(8512, D)
        gfin = part(9536, D)
        xst = part(10656, D, p=(0, T))
        xt = part(11680, KD, T)
        xtf = part(11680, KD * T)
        sg = part(12192, 256)
        hh = part(12448, 256)
        ht = part(12704, 2, P)
        yo = part(12960, 512)
        x2 = part(13472, D)
        x2T = part(15000, KD, P)
        x2T_f = part(15000, D)
        lgs = part(16024, P, p=(0, 36))
        wr = part(20064, KD, 36)
        rt = [16152]

        def small(*shape):
            rt[0] += int(np.prod(shape))
            return part(rt[0] - int(np.prod(shape)), *shape)

        lgt, rexp, og, t4 = small(5, 36), small(5, EG), small(5, EG), small(5, EG)
        o1, o2, t8, lsel = (small(5, EPG) for _ in range(4))
        t32, O1, O2, rank, cn = small(5, E), small(5, E), small(5, E), small(5, E), small(3, E)
        rm, r5, m1_, m2_, rdif = (small(5) for _ in range(5))
        assert rt[0] <= 19040
        G = [part(35120 + 1024 * i, D) for i in range(10)]

        cst = sb("cst", [P, C_N])
        pf = sb("pf", [P, PF_N])
        ones = sb("ones", [P, P])
        Kx = sb("Kx", [P, 16, J, C5])
        dK = sb("dK", [P, 16])
        Hs = Kx[:].rearrange("p a j c -> p (a j c)")[:, 0:D].rearrange("p (h d) -> p h d", d=HD)
        rmsN = Kx[:].rearrange("p a j c -> p (a j c)")[:, D:D + N]
        Aj = sb("Aj", [P, 2, 2, G5])
        sst = sb("sst", [P, NS, G5])
        rec = sb("rec", [P, 2, G5])
        ncp = sb("ncp", [P, XBC, CONV - 1])
        ncs = sb("ncs", [P, XBC, NS])
        scv = sb("scv", [P, CONV - 1, XBC, NS])
        dtb = sb("dtb", [HEADS, 1])
        arow = sb("arow", [P, HEADS])
        dtv = sb("dtv", [P, 5, HEADS])
        dav = sb("dav", [P, 5, HEADS])
        csv = sb("csv", [P, 2, HEADS])
        dev = sb("dev", [P, 2, HEADS])
        aexp = sb("aexp", [P, 8])
        eA = sb("eA", [P, 8, NS])
        dts = sb("dts", [P, 8, NS])
        xds = sb("xds", [P, 8, NS])
        ysm = sb("ysm", [P, NS, 8])
        ssum = sb("ssum", [P, 5])
        idx = sb("idx", [T, IDXC], I32)
        idc = [sb(f"idc{i}", [T, 1], I32) for i in range(RING)]
        cum = sb("cum", [1, E + 1], I32)
        slot = sb("slot", [P, 5, 2], I32)
        place = sb("place", [P, 5, 2], I32)
        tokid = sb("tokid", [P, 5], I32)
        zer = sb("zer", [P, IDXC * T // P], I32)
        gate = sb("gate", [P, 2, 5])
        brc = sb("brc", [36, 1])
        onb = sb("onb", [P, 2, P], BF16)
        Ob = sb("Ob", [P, 5, E], BF16)

        ps = ctx.enter_context(nc.psum_tensor("ps", [P, 8, 512], F32))
        ident = cst[:, C_ID:C_ID + P]
        tri = cst[:, C_TRI:C_TRI + P]

        def bc(ap, axis, n):
            v = ap.unsqueeze(axis)
            return v.broadcast_to([*v.shape[:axis], n, *v.shape[axis + 1:]])

        ld_x = [sem(f"ld_x{i}") for i in range(2)]
        ld_const, ld_s5, ld_stk, ld_misc = sem("ld_const"), sem("ld_s5"), sem("ld_stk"), sem("ld_misc")
        ring_full = [sem(f"ring_full{i}") for i in range(3)]
        wide_done = sem("wide_done")
        wide_free = [sem(f"wide_free{i}") for i in range(2)]
        ones_set, sq_done, ms_done, root_in, root_out = (sem(x) for x in (
            "ones_set", "sq_done", "ms_done", "root_in", "root_out"))
        xn_done = sem("xn_done")
        dve, pool, act = sem("dve_order"), sem("pool_order"), sem("act_order")
        s5_act, s5_dve = sem("s5_act"), sem("s5_dve")
        pow_done, wt_done, wp_done, bb_done, q_done = (sem(x) for x in (
            "pow_done", "wt_done", "wp_done", "bb_done", "q_done"))
        k_mm, k_ev, qt_mm, qt_ev, q_st = (sem(x) for x in ("k_mm", "k_ev", "qt_mm", "qt_ev", "q_st"))
        u_st = [sem(f"u_st{i}") for i in range(2)]
        u_ld, u_zero, h_zero, t_zero, t_ld, h0_ld = (sem(x) for x in (
            "u_ld", "u_zero", "h_zero", "t_zero", "t_ld", "h0_ld"))
        qb_ld = [sem(f"qb_ld{i}") for i in range(2)]
        v_done, v_mm, v_ev = sem("v_done"), sem("v_mm"), sem("v_ev")
        lc_mm, lc_ev = sem("lc_mm"), sem("lc_ev")
        raw_done, conv_done, silu_done = sem("raw_done"), sem("conv_done"), sem("silu_done")
        h_done, y5_mm, y5_ev, y5_st = sem("h_done"), sem("y5_mm"), sem("y5_ev"), sem("y5_st")
        outs = sem("outs")
        s5_out = sem("s5_out")
        dt_mm, dt_ev, dtt_mm, dt_done = sem("dt_mm"), sem("dt_ev"), sem("dtt_mm"), sem("dt_done")
        sa_mm, sa_evd, sa_eva, de_in, de_out = (sem(x) for x in ("sa_mm", "sa_evd", "sa_eva", "de_in", "de_out"))
        cb_mm, l_in, l_exp, e2_done, m_done, cs_done = (sem(x) for x in (
            "cb_mm", "l_in", "l_exp", "e2_done", "m_done", "cs_done"))
        y_mm, y_ev, st_mm, st_ev, z_done, ssm_out = (sem(x) for x in (
            "y_mm", "y_ev", "st_mm", "st_ev", "z_done", "ssm_out"))
        ds_mm, ds_ev, ea_out, bcs_mm, bcs_ev = (sem(x) for x in ("ds_mm", "ds_ev", "ea_out", "bcs_mm", "bcs_ev"))
        h0s_ld = [sem(f"h0s_ld{i}") for i in range(2)]
        h0s_st = [sem(f"h0s_st{i}") for i in range(2)]
        hn_done = sem("hn_done")
        zs_done, gt_done, ys_done = sem("zs_done"), sem("gt_done"), sem("ys_done")
        yraw_ld, smv_done = sem("yraw_ld"), sem("smv_done")
        gelu_done, y2_done = sem("gelu_done"), sem("y2_done")
        wo_ld = [sem(f"wo_ld{i}") for i in range(2)]
        x1_ld, o_mm, o_ev = sem("x1_ld"), sem("o_mm"), sem("o_ev")
        moe_ld, xs_sq, x2_done, x2_st, x2t_mm, x2t_ev, lg_mm, lg_ev, lgt_mm, lg_done = (
            sem(x) for x in ("moe_ld", "xs_sq", "x2_done", "x2_st", "x2t_mm",
                             "x2t_ev", "lg_mm", "lg_ev", "lgt_mm", "lg_done"))
        r_in, r_out, ob_done, rank_mm, slot_done, tok_zero, tok_st, idx_ld = (sem(x) for x in (
            "r_in", "r_out", "ob_done", "rank_mm", "slot_done", "tok_zero", "tok_st", "idx_ld"))
        wg_ld = [sem(f"wg_ld{i}") for i in range(2)]
        wu_ld = [sem(f"wu_ld{i}") for i in range(2)]
        wd_ld = [sem(f"wd_ld{i}") for i in range(2)]
        gath = [sem(f"gath{i}") for i in range(RING)]
        idc_done, staged, xtr, xev, gmm, umm, silu, hr, htr, hev, dmm, yev, yst = (sem(x) for x in (
            "idc_done", "staged", "xtr", "xev", "gmm", "umm", "silu", "hr", "htr", "hev", "dmm", "yev", "yst"))
        gy = [sem(f"gy{i}") for i in range(5)]
        fin_done, fo_done, ye_zero = sem("fin_done"), sem("fo_done"), sem("ye_zero")

        gsrc = a["w_gate"].rearrange("e (p k) n -> e p k n", k=KD)
        usrc = a["w_up"].rearrange("e (p k) n -> e p k n", k=KD)
        dsrc = a["w_down"].rearrange("e (k p) n -> e p k n", k=4)

        def conv_tile(i):
            return 8 + i if i < 4 else i - 4

        def conv_dst(i):
            return xcB[:, i, :] if i < 4 else xcX[:, i - 4, :]

        NW = 36

        def tile_bound(eng, i, least):
            return eng.value_load(cum[0:1, i], min_val=least, max_val=MAXT)

        block = ctx.enter_context(nc.Block())


        @block.sync
        def _(sp):
            sp.dma_start(cst[:], a["consts"]).then_inc(ld_const, 16)
            sp.dma_start(pf[:], a["pf"]).then_inc(ld_const, 16)
            for i in range(2):
                sp.dma_start(xT[:, 4 * i:4 * i + 4, :],
                             a["xT"].rearrange("p (k n) -> p k n", k=KD)[:, 4 * i:4 * i + 4, :]).then_inc(ld_x[i], 16)
            sp.dma_start(part(tmp, 3, G5), a["s5p"].rearrange("p (a g) -> p a g", a=3)).then_inc(ld_s5, 16)
            for s in range(3):
                sp.dma_start(ring[s], a["wi"][s].rearrange("p (k n) -> p k n", k=KD)).then_inc(ring_full[s], 16)
            sp.dma_start(stk, a["s5stk"].rearrange("p (a g c) -> p a g c", a=4, g=G5)).then_inc(ld_stk, 16)
            sp.dma_start(dK[:], a["s5dk"]).then_inc(ld_misc, 16)
            sp.dma_start(scv[:], a["cst_in"].rearrange("p (j k b) -> p j k b", k=XBC, b=NS)).then_inc(ld_misc, 16)
            sp.dma_start(wdt[:], a["wdt"].rearrange("p (k n) -> p k n", k=KD)).then_inc(ld_misc, 16)
            sp.dma_start(dtb[:], a["dtb"]).then_inc(ld_misc, 16)
            sp.dma_start(arow[:], a["alog"].partition_broadcast(P)).then_inc(ld_misc, 16)
            sp.dma_start(brc[:], a["br"]).then_inc(ld_misc, 16)
            sp.dma_start(onb[:], a["onb"].rearrange("p (a q) -> p a q", a=2)).then_inc(ld_misc, 16)
            sp.dma_start(a["o_conv_s"][:, 0:2 * XBC * NS], a["cst_in"][:, XBC * NS:3 * XBC * NS]).then_inc(outs, 16)

            def ring_load(w):
                sp.wait_ge(wide_done, w - 2)
                src = a["wi"][w] if w < 28 else a["wglu"][w - 28]
                sp.dma_start(ring[w % 3], src.rearrange("p (k n) -> p k n", k=KD)).then_inc(ring_full[w % 3], 16)

            for w in (3, 4):
                ring_load(w)
            sp.wait_ge(u_zero, 1)
            for i in range((MAXT - E) * T // P // 4):
                sp.dma_start(ye_scr[E * T + 4 * P * i:E * T + 4 * P * (i + 1), :].rearrange("(p n) d -> p (n d)", p=P),
                             U[:, 0:4 * D]).then_inc(ye_zero, 16)
            for w in (5, 6, 7):
                ring_load(w)
            sp.wait_ge(qt_ev, 1)
            qdst = q_scr.rearrange("(b j) (g r) -> j g b r", j=2, g=G5)
            for j in range(2):
                sp.dma_start(qdst[j], qt[64 * j:64 * j + 64]).then_inc(q_st, 16)
            for w in (8, 9):
                ring_load(w)
            for s in range(2):
                sp.wait_ge(u_st[s], 64)
            sp.wait_ge(ye_zero, 32)
            Ug = U[:, 0:G5 * UC].rearrange("p (g c) -> p g c", g=G5)
            usrc5 = u_scr[:, 0:NP_].rearrange("(g c) (j m) -> j c g m", c=C5, j=J)
            us5 = u_scr[:, NP_:N].rearrange("(g c) b -> c g b", c=C5)
            for j in range(J):
                sp.dma_start(Ug[16 * j:16 * j + 16, :, 0:NC5], usrc5[j]).then_inc(u_ld, 16)
            sp.dma_start(Ug[0:16, :, COL_S0:COL_S0 + NS], us5).then_inc(u_ld, 16)
            sp.dma_start(Ug[16 * (J - 1):16 * J, :, COL_S7:COL_S7 + NS], us5).then_inc(u_ld, 16)
            ring_load(10)

            def qb_loads(half):
                for j in range(J):
                    sp.dma_start(QB[16 * j:16 * j + 16],
                                 q_scr[j, 4096 * half:4096 * half + 4096].partition_broadcast(16)
                                 .rearrange("q (g r s) -> q g r s", g=32, r=2)).then_inc(qb_ld[half], 16)
                    sp.dma_start(BT[16 * j:16 * j + 16],
                                 a["s5bt"][:, 4096 * half:4096 * half + 4096]
                                 .rearrange("q (g r s) -> q g r s", g=32, r=2)).then_inc(qb_ld[half], 16)

            sp.wait_ge(q_st, 32)
            sp.wait_ge(k_mm, 1)
            qb_loads(0)
            for w in (11, 12):
                ring_load(w)
            sp.wait_ge(v_done, 1)
            qb_loads(1)
            for w in (13, 14, 15):
                ring_load(w)

            def toeplitz(r):
                for j in range(J):
                    sp.dma_start(Tm[16 * j:16 * j + 16, r::4, j:J, :],
                                 Kx[32 * r:32 * r + 16, :, 0:J - j, :]).then_inc(t_ld, 16)

            sp.wait_ge(t_zero, 1)
            sp.wait_ge(k_ev, 2)
            toeplitz(0)
            toeplitz(1)
            ring_load(16)
            toeplitz(2)
            toeplitz(3)
            for w in range(17, 22):
                ring_load(w)
            sp.wait_ge(conv_done, XBC)
            sp.dma_start(a["o_conv_p"].rearrange("p (k j) -> p k j", k=XBC), ncp[:]).then_inc(outs, 16)
            sp.dma_start(a["o_conv_s"][:, 2 * XBC * NS:], ncs[:].rearrange("p k b -> p (k b)")).then_inc(outs, 16)
            for w in range(22, 26):
                ring_load(w)
            sp.wait_ge(y5_ev, 16)
            ydst = y_scr[:, 0:NP_].rearrange("(g c) (j m) -> j c g m", c=C5, j=J)
            for j in range(J):
                sp.dma_start(ydst[j], Ug[16 * j:16 * j + 16, :, 0:NC5]).then_inc(y5_st, 16)
            sp.dma_start(y_scr[:, NP_:N].rearrange("(g c) b -> c g b", c=C5),
                         Ug[0:16, :, COL_S0:COL_S0 + NS]).then_inc(y5_st, 16)
            ring_load(26)
            sp.wait_ge(y5_st, 16 * 9)
            sp.dma_start(yraw, y_scr.rearrange("(k p) n -> p k n", p=P)).then_inc(yraw_ld, 16)
            for w in range(27, 31):
                ring_load(w)
            wsrc = a["w_out"].rearrange("(k p) n -> p k n", p=P)

            def wo_load(q):
                sp.dma_start(wo[q % 2], wsrc[:, 8 * (q // 2):8 * (q // 2) + 8,
                                             512 * (q % 2):512 * (q % 2) + 512]).then_inc(wo_ld[q % 2], 16)

            sp.wait_ge(gelu_done, 8)
            wo_load(0)
            sp.wait_ge(st_ev, 5)
            sp.dma_start(a["o_ssm_p"], Hs.rearrange("p h d -> p (h d)")).then_inc(ssm_out, 16)
            for w in range(31, NW):
                ring_load(w)
            sp.wait_ge(y2_done, 8)
            for i, (t0, n) in enumerate(TT):
                sp.dma_start(x1[i][0:n], a["xtok"][t0:t0 + n, :]).then_inc(x1_ld, 16)
            sp.wait_ge(wide_done, NW)
            wo_load(1)
            sp.wait_ge(gt_done, 1)
            sp.dma_start(gffn, a["gffn"].partition_broadcast(P)).then_inc(moe_ld, 16)
            sp.dma_start(gfin, a["gfin"].partition_broadcast(P)).then_inc(moe_ld, 16)
            sp.dma_start(wr, a["wr"].rearrange("p (k n) -> p k n", k=KD)).then_inc(moe_ld, 16)
            for s in range(2):
                sp.wait_ge(h0s_st[s], 64)
            sp.dma_start(Wg[1], gsrc[1]).then_inc(wg_ld[1], 16)
            sp.dma_start(Wu[1], usrc[1]).then_inc(wu_ld[1], 16)
            sp.wait_ge(o_mm, 5)
            wo_load(2)
            sp.wait_ge(ms_done, 3)
            sp.dma_start(Wg[0], gsrc[0]).then_inc(wg_ld[0], 16)
            sp.dma_start(Wu[0], usrc[0]).then_inc(wu_ld[0], 16)
            sp.dma_start(Wd[0], dsrc[0]).then_inc(wd_ld[0], 16)
            sp.wait_ge(o_mm, 10)
            wo_load(3)
            sp.wait_ge(o_mm, 20)
            sp.dma_start(Wd[1], dsrc[1]).then_inc(wd_ld[1], 16)
            sp.wait_ge(slot_done, 1)
            with sp.Fori(1, E // 2) as ep:
                for s in range(2):
                    e = ep * 2 + s
                    done = tile_bound(sp, bass.ds(e - 1, 1), 1)
                    sp.wait_ge(umm, done)
                    sp.dma_start(Wg[s], gsrc[bass.ds(e, 1)].rearrange("a p k n -> (a p) k n")).then_inc(wg_ld[s], 16)
                    sp.dma_start(Wu[s], usrc[bass.ds(e, 1)].rearrange("a p k n -> (a p) k n")).then_inc(wu_ld[s], 16)
                    sp.wait_ge(dmm, done + 1)
                    sp.dma_start(Wd[s], dsrc[bass.ds(e, 1)].rearrange("a p k n -> (a p) k n")).then_inc(wd_ld[s], 16)

        @block.gpsimd
        def _(pl):
            cnt = [0]

            def link(ins):
                cnt[0] += 1
                ins.then_inc(pool, 1)
                pl.wait_ge(pool, cnt[0])

            nc.gpsimd.memset(U, 0.0).then_inc(u_zero, 1)
            nc.gpsimd.memset(zer[:], 0)
            link(nc.gpsimd.iota(tokid[:], [[P, 5]], base=0, channel_multiplier=1))
            pl.dma_start(tok_scr.rearrange("(p n) a -> p (n a)", p=P), zer[:]).then_inc(tok_zero, 16)
            pl.wait_ge(ld_stk, 16)
            pl.wait_ge(pow_done, 1)
            nc.gpsimd.tensor_tensor(Wt, bc(stk[:, 1], 2, J + 1), bc(Pim.rearrange("p t g -> p g t"), 3, C5),
                                    ALU.mult).then_inc(wt_done, 1)
            pl.wait_ge(wp_done, 1)
            HA = part(HA_off, 76, G5)
            nc.gpsimd.memset(HA[:, 75], 0.0)
            nc.gpsimd.memset(HA[:, 0], 0.0).then_inc(h_zero, 1)
            pl.dma_start(HA[:, COL_S0:COL_S0 + NS].rearrange("p b g -> p (b g)"),
                         a["h0s5"].rearrange("r s b -> (r s) b")).then_inc(h0_ld, 16)
            pl.wait_ge(v_done, 2)
            nc.gpsimd.memset(Tm, 0.0).then_inc(t_zero, 1)

            lo, hi = slice(0, 64), slice(64, 128)
            pl.wait_ge(h0_ld, 16)
            pl.wait_ge(v_ev, 16)
            pl.wait_ge(h_zero, 1)
            for c in range(NC5):
                here, nxt = HA[:, c], HA[:, c + 1]
                link(nc.gpsimd.tensor_tensor(rec[:, 0], Aj[:, 0, 0], here, ALU.mult))
                link(nc.gpsimd.tensor_tensor(rec[lo, 1], Aj[hi, 0, 1], here[hi], ALU.mult))
                link(nc.gpsimd.tensor_tensor(rec[hi, 1], Aj[lo, 0, 1], here[lo], ALU.mult))
                link(nc.gpsimd.tensor_tensor(nxt, nxt, rec[:, 0], ALU.add))
                link(nc.gpsimd.tensor_tensor(nxt, nxt, rec[:, 1], ALU.add))
            h0v = HA[:, COL_S0:COL_S0 + NS]
            link(nc.gpsimd.tensor_tensor(smp, bc(Aj[:, 1, 0], 1, NS), h0v, ALU.mult))
            link(nc.gpsimd.tensor_tensor(sst[:], sst[:], smp, ALU.add))
            link(nc.gpsimd.tensor_tensor(smp[lo], bc(Aj[hi, 1, 1], 1, NS), h0v[hi], ALU.mult))
            link(nc.gpsimd.tensor_tensor(smp[hi], bc(Aj[lo, 1, 1], 1, NS), h0v[lo], ALU.mult))
            nc.gpsimd.tensor_tensor(sst[:], sst[:], smp, ALU.add).then_inc(h_done, 1)
            pl.wait_ge(h_done, 1)
            pl.dma_start(a["o_s5p"].rearrange("r s g -> (r s) g"), HA[:, NC5]).then_inc(s5_out, 16)
            pl.dma_start(a["o_s5s"].rearrange("r s g -> (r s) g"), sst[:].rearrange("p b g -> p (b g)")).then_inc(s5_out, 16)

            pl.wait_ge(ea_out, 1)
            pl.wait_ge(y5_mm, 16)
            hin = a["ssm_in"].rearrange("b (i q) n -> b q i n", q=P)
            hout = a["o_ssm_s"].rearrange("b (i q) n -> b q i n", q=P)
            for b in range(2):
                pl.dma_start(h0b[b], hin[b]).then_inc(h0s_ld[b], 16)
            for b in range(NS):
                s = b % 2
                pl.wait_ge(bcs_ev, b + 2)
                link(nc.gpsimd.tensor_tensor(smu.rearrange("p (g i) n -> p g i n", g=2), bc(bcb[b][:, 0:2], 2, 4),
                                             bc(xds[:, :, b].rearrange("p (g i) -> p g i", g=2), 3, NSTATE), ALU.mult))
                pl.wait_ge(h0s_ld[s], 16 * (b // 2 + 1))
                link(nc.gpsimd.tensor_tensor(smt, h0b[s], bc(eA[:, :, b], 2, NSTATE), ALU.mult))
                nc.gpsimd.tensor_tensor(h0b[s], smt, smu, ALU.add).then_inc(hn_done, 1)
                pl.wait_ge(hn_done, b + 1)
                pl.dma_start(hout[b], h0b[s]).then_inc(h0s_st[s], 16)
                if 1 <= b < NS - 1:
                    pl.wait_ge(h0s_st[1 - s], 16 * ((b - 1) // 2 + 1))
                    pl.wait_ge(smv_done, b)
                    pl.dma_start(h0b[1 - s], hin[b + 1]).then_inc(h0s_ld[1 - s], 16)

            pl.wait_ge(slot_done, 1)
            pl.wait_ge(tok_zero, 16)
            for i, (t0, n) in enumerate(TT):
                for k in range(2):
                    nc.gpsimd.indirect_dma_start(tok_scr, bass.IndirectOffsetOnAxis(ap=place[0:n, i, k:k + 1], axis=0),
                                                 tokid[0:n, i:i + 1], None).then_inc(tok_st, 16)
            pl.wait_ge(tok_st, 160)
            pl.dma_start(idx[:], tok_scr.rearrange("(p q) a -> p (q a)", p=T)).then_inc(idx_ld, 16)
            pl.wait_ge(idx_ld, 16)
            pl.wait_ge(x2_st, 80)

            def gather(u, col):
                link(nc.gpsimd.tensor_copy(idc[u][:], idx[:, col]))
                nc.gpsimd.indirect_dma_start(xg[u], None, x2_scr,
                                             bass.IndirectOffsetOnAxis(ap=idc[u][:], axis=0)).then_inc(gath[u], 16)

            for u in range(RING):
                gather(u, slice(u, u + 1))
            nt = tile_bound(pl, slice(E, E + 1), E)
            with pl.Fori(0, (nt + RING) // RING) as it:
                for u in range(RING):
                    pl.wait_ge(xtr, it * RING + u + 1)
                    pl.wait_ge(gath[u], it * 16 + 16)
                    pl.nop(nofuse=True)
                    nc.gpsimd.tensor_copy(xst, xg[u]).then_inc(staged, 1)
                    pl.wait_ge(staged, it * RING + u + 1)
                    pl.nop(nofuse=True)
                    nc.gpsimd.tensor_copy(idc[u][:], idx[:, bass.ds(it * RING + u + RING, 1)]).then_inc(idc_done, 1)
                    pl.wait_ge(idc_done, it * RING + u + 1)
                    pl.nop(nofuse=True)
                    nc.gpsimd.indirect_dma_start(xg[u], None, x2_scr,
                                                 bass.IndirectOffsetOnAxis(ap=idc[u][:], axis=0)).then_inc(gath[u], 16)
            for u in range(RING):
                pl.wait_ge(gath[u], ((nt + RING) // RING) * 16 + 16)
            pl.wait_ge(yst, nt * 32 + 32)
            pl.nop(nofuse=True)
            for i, (t0, n) in enumerate(TT):
                for k in range(2):
                    nc.gpsimd.indirect_dma_start(G[2 * i + k][0:n], None, ye_scr,
                                                 bass.IndirectOffsetOnAxis(ap=slot[0:n, i, k:k + 1], axis=0))\
                        .then_inc(gy[i], 16)

        @block.tensor
        def _(pe):
            mm = nc.tensor.matmul

            def wide(w):
                src = xn if w < 28 else yg
                pe.wait_ge(ring_full[w % 3], 16 * (w // 3 + 1))
                if w >= 2:
                    pe.wait_ge(wide_free[w % 2], w // 2)
                if w == 28:
                    pe.wait_ge(gelu_done, 8)
                b0 = 2 * (w % 2)
                for k in range(KD):
                    if w == 0:
                        pe.wait_ge(xn_done, k + 1)
                    for h, (t0, t1) in enumerate(HALVES):
                        last = mm(ps[:, b0 + h, 0:t1 - t0], ring[w % 3][:, k, :], src[:, k, t0:t1],
                                  start=k == 0, stop=k == KD - 1)
                last.then_inc(wide_done, 1)

            def mean_square(src, done, each):
                for k in range(KD):
                    if each is not None:
                        pe.wait_ge(each, k + 1)
                    for h, (t0, t1) in enumerate(HALVES):
                        last = mm(ps[:, 4 + h, 0:t1 - t0], ones[:], src[:, k, t0:t1], start=k == 0, stop=k == KD - 1)
                last.then_inc(done, 1)

            pe.wait_ge(ones_set, 1)
            mean_square(sq0, ms_done, sq_done)
            for w in range(6):
                wide(w)
            pe.wait_ge(q_done, 1)
            Qf = Qs.rearrange("p j g -> p (j g)")
            for i in range(4):
                last = nc.tensor.transpose(ps[:, 6, i * P:(i + 1) * P], Qf[:, i * P:(i + 1) * P], ident)
            last.then_inc(qt_mm, 1)
            for w in range(6, 8):
                wide(w)
            pe.wait_ge(wp_done, 1)
            pe.wait_ge(bb_done, 1)
            pe.wait_ge(qt_ev, 1)
            for gq in range(16):
                for r in range(4):
                    g = 4 * gq + r
                    last = mm(ps[32 * r:32 * r + 32, 4 + gq // 4, (gq % 4) * P:(gq % 4) * P + P],
                              Bb[:, g * C5:(g + 2) * C5], Wp[:, g, 0:J, :], start=True, stop=True)
            last.then_inc(k_mm, 1)
            for w in range(8, 12):
                wide(w)
            pe.wait_ge(u_ld, 160)
            pe.wait_ge(k_ev, 1)

            def state_inputs(rd):
                if rd % 8 == 0:
                    pe.wait_ge(v_done, rd // 8 + 1)
                if rd >= 2:
                    pe.wait_ge(v_ev, rd - 1)
                for q in range(4):
                    g = 4 * rd + q
                    last = mm(ps[:, 4 + rd % 2, q * WIN:q * WIN + WIN], Vm[:, g % 32], U[:, g * UC:g * UC + WIN],
                              start=True, stop=True)
                last.then_inc(v_mm, 1)

            pe.wait_ge(ld_misc, 112)
            for h, (t0, t1) in enumerate(HALVES):
                for k in range(KD):
                    last = mm(ps[0:HEADS, 6 + h, 0:t1 - t0], wdt[:, k, :], xn[:, k, t0:t1],
                              start=k == 0, stop=k == KD - 1)
            last.then_inc(dt_mm, 1)
            for rd in range(8):
                state_inputs(rd)
            for w in (12, 13):
                wide(w)
            for rd in range(8, 16):
                state_inputs(rd)
            pe.wait_ge(dt_ev, 1)
            for i, (t0, n) in enumerate(TT):
                last = nc.tensor.transpose(ps[0:n, 6, i * HEADS:(i + 1) * HEADS], dt_raw[:, t0:t0 + n],
                                           cst[0:HEADS, C_ID:C_ID + HEADS])
            last.then_inc(dtt_mm, 1)
            for w in range(14, 20):
                wide(w)
            pe.wait_ge(t_ld, 16 * 32)
            pe.wait_ge(v_ev, 16)
            for rd in range(16):
                if rd >= 2:
                    pe.wait_ge(lc_ev, rd - 1)
                for q in range(4):
                    g = 4 * rd + q
                    last = mm(ps[:, 4 + rd % 2, q * WIN:q * WIN + WIN], Tm[:, g], U[:, g * UC:g * UC + WIN],
                              start=True, stop=True)
                last.then_inc(lc_mm, 1)
            pe.wait_ge(dt_done, 1)
            for h in range(HEADS):
                r, i = h % 2, h // 2
                last = mm(ps[64 * r:64 * r + 64, 6, 256 + i * NS:256 + (i + 1) * NS],
                          dtv[0:24, 4, h:h + 1].broadcast_to([24, HD]), cst[0:24, C_ID + 16:C_ID + 24],
                          start=True, stop=True)
            last.then_inc(ds_mm, 1)
            pe.wait_ge(ds_ev, 1)
            pe.wait_ge(lc_ev, 16)

            def state_outputs():
                pe.wait_ge(h_done, 1)
                pe.wait_ge(y_ev, 2)
                HAv = arena[:, HA_off:HA_off + WIN * G5].rearrange("p (c g) -> p g c", g=G5)
                for rd in range(16):
                    if rd >= 2:
                        pe.wait_ge(y5_ev, rd - 1)
                    for q in range(4):
                        g = 4 * rd + q
                        last = mm(ps[:, 4 + rd % 2, q * WIN:q * WIN + WIN], Wp[:, g, 1:J + 1, :], HAv[:, g, :],
                                  start=True, stop=True)
                    last.then_inc(y5_mm, 1)

            def sample_bc():
                pe.wait_ge(st_ev, 2)
                for i in range(4):
                    last = nc.tensor.transpose(ps[0:24, 7, i * P:(i + 1) * P], xcB[:, i, 4 * P:N], ident)
                last.then_inc(bcs_mm, 1)
                pe.wait_ge(y5_ev, 16)
                for b in range(NS):
                    pe.wait_ge(bcs_ev, max(1, b - 2))
                    mm(ps[:, 4 + b % 4, :], cst[0:24, C_ID + 16 + b:C_ID + 17 + b].broadcast_to([24, P]), bts[0:24],
                       start=True, stop=True).then_inc(bcs_mm, 1)
                pe.wait_ge(bcs_ev, 9)

            def ssd_a(c):
                t0, n = CH[c]
                if c >= 1:
                    pe.wait_ge(y_ev, c)
                    pe.wait_ge(st_ev, c)
                for i in range(8):
                    nc.tensor.transpose(ps[0:n, 4 + i // 4, (i % 4) * P:(i % 4 + 1) * P], xcX[:, i, t0:t0 + n], ident)
                for i in range(2):
                    nc.tensor.transpose(ps[0:n, 6, i * P:(i + 1) * P], xcB[:, i, t0:t0 + n], ident)
                mm(ps[0:n, 7, 0:16], tri[0:n, 0:n], dav[0:n, c, :], start=True, stop=True)
                mm(ps[:, 7, 16:32], ones[0:n, :], dav[0:n, c, :], start=True, stop=True)
                for g in range(2):
                    last = mm(ps[0:n, 7, 128 + g * P:128 + g * P + n], xcB[:, g, t0:t0 + n], xcB[:, 2 + g, t0:t0 + n],
                              start=True, stop=True)
                last.then_inc(sa_mm, 1)

            def ssd_b(c):
                n = CH[c][1]
                pe.wait_ge(sa_evd, c + 1)
                pe.wait_ge(sa_eva, c + 1)
                for h in range(HEADS):
                    last = mm(ps[:, 4 + h // 4, (h % 4) * P:(h % 4) * P + n],
                              dav[0:n, c, h:h + 1].broadcast_to([n, P]), tri[0:n, 0:n], start=True, stop=True)
                last.then_inc(cb_mm, 1)

            def ssd_c(c):
                n = CH[c][1]
                pe.wait_ge(m_done, c + 1)
                if c:
                    pe.wait_ge(cs_done, c)
                for i in range(8):
                    for r in range(2):
                        h = 2 * i + r
                        last = mm(ps[64 * r:64 * r + 64, 4 + i // 4, (i % 4) * P:(i % 4) * P + n],
                                  xdt[0:n, h, :], Lm[0:n, h, 0:n], start=True, stop=c == 0)
                    for r in range(2) if c else ():
                        h = 2 * i + r
                        last = mm(ps[64 * r:64 * r + 64, 4 + i // 4, (i % 4) * P:(i % 4) * P + n],
                                  Hs[:, h, :], E2[:, h, 0:n], start=False, stop=True)
                last.then_inc(y_mm, 1)
                for g in range(2):
                    last = mm(ps[:, 6 + g, :], btok[0:n, g, :], xde[0:n, 8 * g:8 * g + 8, :], start=True, stop=True)
                last.then_inc(st_mm, 1)

            pe.wait_ge(silu_done, XBC)
            for c in range(5):
                ssd_a(c)
                if c < 4:
                    wide(20 + 2 * c)
                ssd_b(c)
                if c < 4:
                    wide(21 + 2 * c)
                ssd_c(c)
                if c == 1:
                    state_outputs()
                    sample_bc()
            for w in range(28, 32):
                wide(w)
            pe.wait_ge(sq_done, 16)
            mean_square(sq, ms_done, None)
            for w in range(32, 36):
                wide(w)

            def project(q):
                src = ySSD if q < 2 else sig
                pe.wait_ge(wo_ld[q % 2], 16 * (q // 2 + 1))
                for i, (t0, n) in enumerate(TT):
                    o = 5 * q + i
                    if o >= 4:
                        pe.wait_ge(o_ev, o - 3)
                    for k in range(KD):
                        last = mm(ps[0:n, o % 4, :], src[:, k, t0:t0 + n], wo[q % 2][:, k, :], start=k == 0, stop=k == KD - 1)
                    last.then_inc(o_mm, 1)

            pe.wait_ge(wide_free[0], 18)
            pe.wait_ge(wide_free[1], 18)
            pe.wait_ge(ys_done, 1)
            project(0)
            pe.wait_ge(sq_done, 24)
            mean_square(sq, ms_done, None)
            project(1)
            pe.wait_ge(ys_done, 2)
            project(2)
            project(3)

            pe.wait_ge(moe_ld, 48)
            for i, (t0, n) in enumerate(TT):
                pe.wait_ge(x2_done, i + 1)
                if i == 0:
                    pe.wait_ge(ys_done, 2)
                else:
                    pe.wait_ge(x2t_ev, i)
                for k in range(KD):
                    last = nc.tensor.transpose(ps[:, 4 + k // 4, (k % 4) * P:(k % 4) * P + n], x2[0:n, k * P:(k + 1) * P],
                                               cst[0:n, C_ID:C_ID + n])
                last.then_inc(x2t_mm, 1)
                pe.wait_ge(x2t_ev, i + 1)
                for k in range(KD):
                    last = mm(ps[0:36, 6, 0:n], wr[:, k, :], x2T[:, k, 0:n], start=k == 0, stop=k == KD - 1)
                last.then_inc(lg_mm, 1)
                pe.wait_ge(lg_ev, i + 1)
                nc.tensor.transpose(ps[0:n, 7, i * 36:(i + 1) * 36], lgs[:, 0:n], cst[0:36, C_ID:C_ID + 36]).then_inc(lgt_mm, 1)
            pe.wait_ge(ob_done, 1)
            for i in range(6):
                for j in range(min(i, 4) + 1):
                    last = mm(ps[:, 7, 256 + i * E:256 + (i + 1) * E], onb[:, 1 if j == i else 0, :], Ob[:, j, :],
                              start=j == 0, stop=j == min(i, 4))
            last.then_inc(rank_mm, 1)

            def x_transposes(q):
                pe.wait_ge(staged, q + 1)
                pe.nop(nofuse=True)
                for k in range(KD):
                    last = nc.tensor.transpose(ps[:, 2, k * T:(k + 1) * T], xst[:, k::KD], cst[0:T, C_ID:C_ID + T])
                last.then_inc(xtr, 1)

            pe.wait_ge(slot_done, 1)
            for s_ in (xtr, htr, dmm):
                pe.sem_inc(s_, 1)
            x_transposes(0)
            with pe.Fori(0, E // 2) as ep:
                for s in range(2):
                    e = ep * 2 + s
                    q0 = tile_bound(pe, bass.ds(e, 1), 0)
                    q1 = tile_bound(pe, bass.ds(e + 1, 1), 1)
                    with pe.Fori(q0, q1) as q:
                        pe.wait_ge(xev, q + 1)
                        pe.wait_ge(wg_ld[s], ep * 16 + 16)
                        pe.wait_ge(silu, q + 1)
                        for k in range(KD):
                            for r in range(2):
                                last = mm(ps[64 * r:64 * r + 64, 0, 0:256], xt[:, k, :],
                                          Wg[s][:, k, 256 * r:256 * r + 256], start=k == 0, stop=k == KD - 1)
                        last.then_inc(gmm, 1)
                        pe.wait_ge(wu_ld[s], ep * 16 + 16)
                        pe.wait_ge(hr, q + 1)
                        for k in range(KD):
                            for r in range(2):
                                last = mm(ps[64 * r:64 * r + 64, 1, 0:256], xt[:, k, :],
                                          Wu[s][:, k, 256 * r:256 * r + 256], start=k == 0, stop=k == KD - 1)
                        last.then_inc(umm, 1)
                        x_transposes(q + 1)
                        pe.wait_ge(hr, q + 2)
                        pe.nop(nofuse=True)
                        for j in range(2):
                            last = nc.tensor.transpose(ps[:, 3, j * P:(j + 1) * P], hh[:, j * P:(j + 1) * P], ident)
                        last.then_inc(htr, 1)
                        pe.wait_ge(hev, q + 1)
                        pe.wait_ge(wd_ld[s], ep * 16 + 16)
                        pe.wait_ge(yev, q + 1)
                        for k in range(4):
                            for r in range(2):
                                last = mm(ps[64 * r:64 * r + 64, 4, :], ht[:, k % 2, 64 * (k // 2):64 * (k // 2) + 64],
                                          Wd[s][:, k, 512 * r:512 * r + 512], start=k == 0, stop=k == 3)
                        last.then_inc(dmm, 1)
            pe.sem_inc(xtr, 3)

        @block.scalar
        def _(ac):
            act_ = nc.scalar.activation
            cnt = [0]

            def link(ins):
                cnt[0] += 1
                ins.then_inc(act, 1)
                ac.wait_ge(act, cnt[0])

            for k in range(KD):
                if k % 4 == 0:
                    ac.wait_ge(ld_x[k // 4], 16)
                act_(sq0[:, k, :], xT[:, k, :], ACT.Square).then_inc(sq_done, 1)
            ac.wait_ge(root_in, 1)
            act_(rms0, rms0, ACT.Sqrt).then_inc(root_out, 1)
            ac.wait_ge(ld_s5, 16)
            act_(tv(3), tv(2), ACT.Exp).then_inc(s5_act, 1)
            ac.wait_ge(s5_dve, 1)
            act_(tv(5), tv(4), ACT.Exp).then_inc(s5_act, 1)
            ac.wait_ge(s5_dve, 2)
            act_(tv(8), tv(6), ACT.Sin).then_inc(s5_act, 1)
            act_(tv(9), tv(7), ACT.Sin).then_inc(s5_act, 1)

            def evac_u(w):
                ac.wait_ge(wide_done, w + 1)
                if w >= 2:
                    ac.wait_ge(u_st[w % 2], 16 * (w // 2))
                b0 = 2 * (w % 2)
                dst = uD[w % 2]
                dj = dst[:, 0:NP_].rearrange("p (j m) -> p j m", j=J)
                act_(dj[:, :, 0:33], ps[:, b0, 0:SPLIT].rearrange("p (m j) -> p j m", j=J), ACT.Copy)
                act_(dj[:, :, 33:66], ps[:, b0 + 1, 0:SPLIT].rearrange("p (m j) -> p j m", j=J), ACT.Copy)
                act_(dst[:, NP_:N], ps[:, b0 + 1, SPLIT:N - SPLIT], ACT.Copy).then_inc(wide_free[w % 2], 1)
                ac.wait_ge(wide_free[w % 2], w // 2 + 1)
                ac.dma_start(u_scr[w * P:(w + 1) * P, :], dst).then_inc(u_st[w % 2], 16)

            for w in range(8):
                evac_u(w)
            ac.wait_ge(k_mm, 1)
            for i in range(4):
                last = act_(Kx[:, 4 * i:4 * i + 4], ps[:, 4 + i, :].rearrange("p (q j c) -> p q j c", q=4, j=J), ACT.Copy)
            last.then_inc(k_ev, 1)

            def raw_evac(w):
                i = w - 8
                ac.wait_ge(wide_done, w + 1)
                if i >= 2:
                    ac.wait_ge(conv_done, i - 1)
                b0 = 2 * (w % 2)
                dst = raw[i % 2]
                act_(dst[:, 3:3 + SPLIT], ps[:, b0, 0:SPLIT], ACT.Copy)
                act_(dst[:, 3 + SPLIT:3 + NP_], ps[:, b0 + 1, 0:SPLIT], ACT.Copy)
                sm = dst[:, 531:563].rearrange("p (b j) -> p b j", j=CONV)
                act_(sm[:, :, 3], ps[:, b0 + 1, SPLIT:N - SPLIT], ACT.Copy).then_inc(wide_free[w % 2], 1)
                f = conv_tile(i)
                act_(sm[:, :, 0:3].rearrange("p b j -> p j b"), scv[:, :, f, :], ACT.Copy).then_inc(raw_done, 1)

            def conv_silu(i):
                ac.wait_ge(conv_done, i + 1)
                dst = conv_dst(i)
                act_(dst, dst, ACT.Silu).then_inc(silu_done, 1)

            ac.wait_ge(ld_misc, 112)
            for i in range(4):
                raw_evac(8 + i)
                if i:
                    conv_silu(i - 1)
            conv_silu(3)

            def states_evac(rd):
                ac.wait_ge(v_mm, rd + 1)
                src = ps[:, 4 + rd % 2, 0:4 * WIN].rearrange("p (q c) -> p q c", q=4)
                act_(part(HA_off, 76, G5)[:, 1:67, 4 * rd:4 * rd + 4].rearrange("p c g -> p g c"), src[:, :, 0:NC5], ACT.Copy)
                act_(sst[:, :, 4 * rd:4 * rd + 4].rearrange("p c g -> p g c"), src[:, :, COL_S7:COL_S7 + NS],
                     ACT.Copy).then_inc(v_ev, 1)

            for rd in range(8):
                states_evac(rd)
            for i in (4, 5):
                raw_evac(8 + i)
            for rd in range(8, 16):
                states_evac(rd)
            ac.wait_ge(s5_dve, 3)
            act_(sp_u, sp_u, ACT.Exp)
            act_(arow[:], arow[:], ACT.Exp)
            act_(aexp[:], pf[:, PF_ALOG:PF_ALOG + 8], ACT.Exp).then_inc(s5_act, 1)
            conv_silu(4)
            for i in range(6, XBC):
                raw_evac(8 + i)
                conv_silu(i - 1)
            conv_silu(XBC - 1)
            Ug = U[:, 0:G5 * UC].rearrange("p (g c) -> p g c", g=G5)
            for rd in range(16):
                ac.wait_ge(lc_mm, rd + 1)
                act_(Ug[:, 4 * rd:4 * rd + 4, 0:YC],
                     ps[:, 4 + rd % 2, 0:4 * WIN].rearrange("p (q c) -> p q c", q=4)[:, :, 0:YC], ACT.Copy).then_inc(lc_ev, 1)
            ac.wait_ge(ds_ev, 1)
            act_(eA[:], eA[:], ACT.Exp).then_inc(ea_out, 1)

            def z_evac(w):
                ac.wait_ge(wide_done, w + 1)
                b0 = 2 * (w % 2)
                act_(zT[:, w - 20, 0:SPLIT], ps[:, b0, 0:SPLIT], ACT.Copy)
                act_(zT[:, w - 20, SPLIT:N], ps[:, b0 + 1, 0:N - SPLIT], ACT.Copy).then_inc(wide_free[w % 2], 1)

            for c in range(5):
                n = CH[c][1]
                ac.wait_ge(sa_mm, c + 1)
                act_(btok[0:n], ps[0:n, 6, 0:2 * P].rearrange("p (a q) -> p a q", a=2), ACT.Copy).then_inc(sa_eva, 1)
                ac.wait_ge(de_in, c + 1)
                act_(dev[:], dev[:], ACT.Exp).then_inc(de_out, 1)
                if c < 4:
                    z_evac(20 + 2 * c)
                ac.wait_ge(cb_mm, c + 1)
                for i in range(4):
                    ac.wait_ge(l_in, 4 * c + i + 1)
                    last = act_(E2[:, 4 * i:4 * i + 4, 0:n],
                                ps[:, 4 + i, :].rearrange("p (h l) -> p h l", h=4)[:, :, 0:n], ACT.Exp)
                last.then_inc(e2_done, 1)
                act_(Lm[0:n, :, 0:n], Lm[0:n, :, 0:n], ACT.Exp).then_inc(l_exp, 1)
                if c < 4:
                    z_evac(21 + 2 * c)
                if c == 1:
                    ac.wait_ge(bcs_mm, 1)
                    ac.wait_ge(s5_out, 32)
                    act_(bts[0:24], ps[0:24, 7, :].rearrange("p (a q) -> p a q", a=4), ACT.Copy).then_inc(bcs_ev, 1)
                    for b in range(NS):
                        ac.wait_ge(bcs_mm, b + 2)
                        act_(bcb[b], ps[:, 4 + b % 4, :].rearrange("p (a q) -> p a q", a=4), ACT.Copy).then_inc(bcs_ev, 1)
                if c == 3:
                    ac.wait_ge(yraw_ld, 16)
                    for i in range(8):
                        act_(yg[:, i, 0:NP_].rearrange("p (m j) -> p m j", j=J),
                             yraw[:, i, 0:NP_].rearrange("p (j m) -> p m j", j=J), ACT.Gelu_apprx_tanh)
                        act_(yg[:, i, NP_:N], yraw[:, i, NP_:N], ACT.Gelu_apprx_tanh).then_inc(gelu_done, 1)
            act_(zT, zT, ACT.Silu).then_inc(zs_done, 1)

            ac.wait_ge(gt_done, 1)
            for k in range(KD):
                act_(sq[:, k, :], ySSD[:, k, :], ACT.Square).then_inc(sq_done, 1)

            def norm_root(i):
                ac.wait_ge(root_in, i + 2)
                act_(rmsN, rmsN, ACT.Sqrt).then_inc(root_out, 1)

            for w in range(28, 36):
                ac.wait_ge(wide_done, w + 1)
                b0 = 2 * (w % 2)
                i = w - 28
                act_(sig[:, i, 0:SPLIT], ps[:, b0, 0:SPLIT], ACT.Sigmoid, bias=pf[:, PF_BGLU + i:PF_BGLU + i + 1])
                act_(sig[:, i, SPLIT:N], ps[:, b0 + 1, 0:N - SPLIT], ACT.Sigmoid,
                     bias=pf[:, PF_BGLU + i:PF_BGLU + i + 1]).then_inc(wide_free[w % 2], 1)
                if w == 31:
                    norm_root(0)
            ac.wait_ge(ys_done, 1)
            for k in range(KD):
                ac.wait_ge(y2_done, k + 1)
                act_(sq[:, k, :], sig[:, k, :], ACT.Square).then_inc(sq_done, 1)
            norm_root(1)

            for i, (t0, n) in enumerate(TT):
                ac.wait_ge(o_ev, 15 + i + 1)
                if i:
                    ac.wait_ge(xs_sq, i)
                act_(x2T_f[0:n], x1[i][0:n], ACT.Square, accum_out=ssum[0:n, i:i + 1]).then_inc(xs_sq, 1)
            ac.wait_ge(root_in, 4)
            act_(ssum[:], ssum[:], ACT.Sqrt).then_inc(root_out, 1)
            for i, (t0, n) in enumerate(TT):
                ac.wait_ge(x2_done, i + 1)
                ac.dma_start(x2_scr[t0:t0 + n, :], x2[0:n, :]).then_inc(x2_st, 16)
                ac.wait_ge(x2t_mm, i + 1)
                for h in range(2):
                    last = act_(x2T[:, 4 * h:4 * h + 4, 0:n],
                                ps[:, 4 + h, :].rearrange("p (k t) -> p k t", k=4)[:, :, 0:n], ACT.Copy)
                last.then_inc(x2t_ev, 1)
                ac.wait_ge(lg_mm, i + 1)
                if i:
                    ac.wait_ge(lgt_mm, i)
                act_(lgs[:, 0:n], ps[0:36, 6, 0:n], ACT.Identity, bias=brc[:]).then_inc(lg_ev, 1)
            ac.wait_ge(r_in, 1)
            act_(rexp, rexp, ACT.Exp).then_inc(r_out, 1)
            ac.wait_ge(r_in, 2)
            act_(rdif, rdif, ACT.Exp).then_inc(r_out, 1)

            ac.wait_ge(slot_done, 1)
            ac.wait_ge(ye_zero, 32)
            nt = tile_bound(ac, slice(E, E + 1), E)
            for s_, v_ in ((silu, 1), (yev, 1), (yst, 32)):
                ac.sem_inc(s_, v_)
            with ac.Fori(0, nt) as q:
                ac.wait_ge(gmm, q + 1)
                ac.wait_ge(hr, q + 1)
                act_(sg, ps[:, 0, 0:256], ACT.Silu).then_inc(silu, 1)
                ac.wait_ge(dmm, q + 2)
                ac.wait_ge(yst, q * 32 + 32)
                act_(yo, ps[:, 4, :], ACT.Copy).then_inc(yev, 1)
                ac.wait_ge(yev, q + 2)
                for r in range(2):
                    ac.dma_start(ye_scr[bass.ds(q * T, T), r * 512:r * 512 + 512], yo[64 * r:64 * r + 64, :]).then_inc(yst, 16)
                ac.nop(nofuse=True)
            ac.nop(nofuse=True)
            for i, (t0, n) in enumerate(TT):
                ac.wait_ge(fin_done, i + 1)
                act_(G[2 * i][0:n], x1[i][0:n], ACT.Square, accum_out=ssum[0:n, i:i + 1]).then_inc(xs_sq, 1)
            ac.wait_ge(root_in, 5)
            act_(ssum[:], ssum[:], ACT.Sqrt).then_inc(root_out, 1)
            for i, (t0, n) in enumerate(TT):
                ac.wait_ge(fo_done, i + 1)
                ac.dma_start(a["o_y"][t0:t0 + n, :], x1[i][0:n]).then_inc(outs, 16)
            for s in range(2):
                ac.wait_ge(h0s_st[s], 64)
            ac.wait_ge(s5_out, 32)
            ac.wait_ge(ssm_out, 16)
            ac.wait_ge(outs, 16 * 8)

        @block.vector
        def _(dv):
            V = nc.vector
            cnt = [0]

            def link(ins):
                cnt[0] += 1
                ins.then_inc(dve, 1)
                dv.wait_ge(dve, cnt[0])

            def tt(o, x, y, op):
                link(V.tensor_tensor(o, x, y, op))

            def ts(o, x, s1, s2, op0, op1=None):
                if op1 is None:
                    link(V.tensor_scalar(o, x, s1, None, op0))
                else:
                    link(V.tensor_scalar(o, x, s1, s2, op0, op1))

            def stt(o, x, s, y, op0, op1):
                link(V.scalar_tensor_tensor(o, x, s, y, op0, op1))

            V.memset(ones[:], 1.0).then_inc(ones_set, 1)
            V.memset(raw[0][:, 0:3], 0.0)
            V.memset(raw[1][:, 0:3], 0.0)
            link(V.memset(dtv[:], 0.0))
            link(V.memset(ssum[:], 0.0))
            dv.wait_ge(ld_const, 32)

            def root(rms, want):
                for h, (t0, t1) in enumerate(HALVES):
                    last = V.tensor_scalar(rms[:, t0:t1], ps[:, 4 + h, 0:t1 - t0], 1.0 / D, EPS, ALU.mult, ALU.add)
                last.then_inc(root_in, 1)
                dv.wait_ge(root_out, want)
                link(V.reciprocal(rms, rms))

            dv.wait_ge(ms_done, 1)
            root(rms0, 1)
            link(V.memset(dev[:], 0.0))
            for k in range(KD):
                V.scalar_tensor_tensor(xn[:, k, :], xT[:, k, :], pf[:, PF_GMIX + k:PF_GMIX + k + 1], rms0,
                                       ALU.mult, ALU.mult).then_inc(xn_done, 1)
            dv.wait_ge(s5_act, 1)
            tt(tv(4), tv(0), tv(3), ALU.mult)
            V.tensor_tensor(tv(10), tv(1), tv(3), ALU.mult).then_inc(s5_dve, 1)
            dv.wait_ge(s5_dve, 1)
            ts(tv(11), tv(10), 1.0 / (2 * np.pi), MAGIC, ALU.mult, ALU.add)
            ts(tv(11), tv(11), MAGIC, None, ALU.subtract)
            for part_of in (TWO_PI_HI, TWO_PI_MID, TWO_PI_LO):
                stt(tv(10), tv(11), -float(part_of), tv(10), ALU.mult, ALU.add)
            ts(tv(6), tv(10), PI_F, -PI_F, ALU.min, ALU.max)
            ts(tv(7), tv(6), -1.0, None, ALU.mult)
            tt(tv(7), tv(7), tv(6), ALU.max)
            V.tensor_scalar(tv(7), tv(7), -1.0, float(np.pi / 2), ALU.mult, ALU.add).then_inc(s5_dve, 1)
            dv.wait_ge(s5_act, 4)
            tt(Pre[:, 1, :], tv(5), tv(9), ALU.mult)
            tt(Pim[:, 1, :], tv(5), tv(8), ALU.mult)
            link(V.memset(Pre[:, 0, :], 1.0))
            link(V.memset(Pim[:, 0, :], 0.0))
            ts(tv(4), Pre[:, 1, :], 1.0, None, ALU.subtract)
            tt(tv(5), tv(0), tv(0), ALU.mult)
            tt(tv(6), tv(1), tv(1), ALU.mult)
            tt(tv(5), tv(5), tv(6), ALU.add)
            link(V.reciprocal(tv(5), tv(5)))
            tt(tv(6), tv(4), tv(0), ALU.mult)
            tt(tv(7), Pim[:, 1, :], tv(1), ALU.mult)
            tt(tv(6), tv(6), tv(7), ALU.add)
            tt(tv(8), tv(6), tv(5), ALU.mult)
            tt(tv(6), Pim[:, 1, :], tv(0), ALU.mult)
            tt(tv(7), tv(4), tv(1), ALU.mult)
            tt(tv(6), tv(6), tv(7), ALU.subtract)
            tt(tv(9), tv(6), tv(5), ALU.mult)
            for m in (1, 2, 4):
                lo, hi = slice(1, m + 1), slice(m + 1, 2 * m + 1)
                br, bi = bc(Pre[:, m, :], 1, m), bc(Pim[:, m, :], 1, m)
                w0 = pw_t[:, 0:m * G5].rearrange("p (t g) -> p t g", g=G5)
                tt(Pre[:, hi], Pre[:, lo], br, ALU.mult)
                tt(w0, Pim[:, lo], bi, ALU.mult)
                tt(Pre[:, hi], Pre[:, hi], w0, ALU.subtract)
                tt(Pim[:, hi], Pre[:, lo], bi, ALU.mult)
                tt(w0, Pim[:, lo], br, ALU.mult)
                tt(Pim[:, hi], Pim[:, hi], w0, ALU.add)
            V.memset(csv[:], 0.0).then_inc(pow_done, 1)
            sgn, m0, m1 = (cst[:, x:x + 1] for x in (C_SGN, C_M0, C_M1))
            for o, m in enumerate((J, 1)):
                link(V.tensor_copy(Aj[:, o, 0, :], Pre[:, m, :]))
                ts(Aj[:, o, 1, :], Pim[:, m, :], sgn, None, ALU.mult)
            ts(tv(4), tv(8), m0, None, ALU.mult)
            stt(tv(4), tv(9), m1, tv(4), ALU.mult, ALU.add)
            ts(tv(5), tv(8), m1, None, ALU.mult)
            ts(tv(6), tv(9), m0, None, ALU.mult)
            tt(tv(5), tv(5), tv(6), ALU.subtract)
            for j in range(J):
                tt(Qs[:, j, :], Pre[:, J - 1 - j, :], tv(4), ALU.mult)
                tt(tv(7), Pim[:, J - 1 - j, :], tv(5), ALU.mult)
                tt(Qs[:, j, :], Qs[:, j, :], tv(7), ALU.add)
            V.memset(csv[:], 0.0).then_inc(q_done, 1)
            dv.wait_ge(ld_stk, 16)
            ts(tv(6), tv(9), sgn, -1.0, ALU.mult, ALU.mult)
            tt(stk[:, 2], stk[:, 2], bc(tv(8), 2, C5), ALU.mult)
            tt(stk[:, 3], stk[:, 3], bc(tv(6), 2, C5), ALU.mult)
            V.tensor_tensor(stk[:, 2], stk[:, 2], stk[:, 3], ALU.add).then_inc(bb_done, 1)
            ts(stk[:, 0], stk[:, 0], sgn, None, ALU.mult)
            tt(Wp, bc(stk[:, 0], 2, J + 1), bc(Pre.rearrange("p t g -> p g t"), 3, C5), ALU.mult)
            dv.wait_ge(wt_done, 1)
            V.tensor_tensor(Wp, Wp, Wt, ALU.subtract).then_inc(wp_done, 1)
            dv.wait_ge(ld_misc, 112)
            for r in range(4):
                q_ = slice(32 * r, 32 * r + 32)
                tt(dkt[q_], bc(cst[q_, C_ID + 32 * r:C_ID + 32 * r + C5], 1, 16), bc(dK[q_, :], 2, C5), ALU.mult)
            dv.wait_ge(qt_mm, 1)
            V.tensor_copy(qt, ps[:, 6, :].rearrange("p (b r) -> p b r", b=4)).then_inc(qt_ev, 1)
            dv.wait_ge(k_ev, 1)
            V.tensor_tensor(Kx[:, :, 0, :], Kx[:, :, 0, :], dkt, ALU.add).then_inc(k_ev, 1)

            def make_v(half):
                dv.wait_ge(qb_ld[half], 256)
                if half:
                    dv.wait_ge(v_mm, 8)
                tt(Vm, QB, BT, ALU.mult)
                tt(Vm[:, :, 0, :], Vm[:, :, 0, :], Vm[:, :, 1, :], ALU.subtract)
                tt(QB, QB, BT[:, :, ::-1, :], ALU.mult)
                V.tensor_tensor(Vm[:, :, 1, :], QB[:, :, 0, :], QB[:, :, 1, :], ALU.add).then_inc(v_done, 1)

            def conv(i):
                f = conv_tile(i)
                src, dst = raw[i % 2], conv_dst(i)
                w_ = [pf[:, PF_CW + 4 * f + k:PF_CW + 4 * f + k + 1] for k in range(CONV)]
                b_ = pf[:, PF_CB + f:PF_CB + f + 1]
                sm = src[:, 531:563].rearrange("p (b j) -> p b j", j=CONV)
                dv.wait_ge(raw_done, i + 1)
                ts(dst[:, 0:NP_], src[:, 0:NP_], w_[0], b_, ALU.mult, ALU.add)
                ts(dst[:, NP_:N], sm[:, :, 0], w_[0], b_, ALU.mult, ALU.add)
                for k in range(1, CONV):
                    stt(dst[:, 0:NP_], src[:, k:k + NP_], w_[k], dst[:, 0:NP_], ALU.mult, ALU.add)
                    stt(dst[:, NP_:N], sm[:, :, k], w_[k], dst[:, NP_:N], ALU.mult, ALU.add)
                link(V.tensor_copy(ncp[:, f, :], src[:, NP_:NP_ + 3]))
                V.tensor_copy(ncs[:, f], sm[:, :, 3]).then_inc(conv_done, 1)

            conv(0)
            conv(1)
            make_v(0)
            conv(2)
            conv(3)
            make_v(1)
            dv.wait_ge(dt_mm, 1)
            for h, (t0, t1) in enumerate(HALVES):
                link(V.tensor_scalar(dt_raw[:, t0:t1], ps[0:HEADS, 6 + h, 0:t1 - t0], dtb[:], None, ALU.add))
            V.memset(csv[:], 0.0).then_inc(dt_ev, 1)
            dv.wait_ge(dtt_mm, 1)
            link(V.tensor_copy(dtv[:, 0:4, :], ps[:, 6, 0:64].rearrange("p (i h) -> p i h", i=4)))
            link(V.tensor_copy(dtv[0:24, 4, :], ps[0:24, 6, 64:80]))
            dvf, sps, spz = dtv[:].rearrange("p i h -> p (i h)"), sp_s, sp_z
            ts(sp_u, dvf, -1.0, None, ALU.mult)
            V.tensor_tensor(sp_u, sp_u, dvf, ALU.min).then_inc(s5_dve, 1)
            dv.wait_ge(s5_act, 5)
            ts(sps, sp_u, 2.0, None, ALU.add)
            link(V.reciprocal(sps, sps))
            tt(sps, sps, sp_u, ALU.mult)
            tt(spz, sps, sps, ALU.mult)
            link(V.memset(sp_u, 1.0 / 17))
            for m in (15, 13, 11, 9, 7, 5, 3):
                tt(sp_u, sp_u, spz, ALU.mult)
                ts(sp_u, sp_u, 1.0 / m, None, ALU.add)
            tt(sp_u, sp_u, spz, ALU.mult)
            ts(sp_u, sp_u, 1.0, 2.0, ALU.add, ALU.mult)
            tt(sp_u, sp_u, sps, ALU.mult)
            ts(dvf, dvf, 0.0, None, ALU.max)
            tt(dvf, dvf, sp_u, ALU.add)
            tt(dav[:], dtv[:], bc(arow[:], 1, 5), ALU.mult)
            V.tensor_scalar(dav[:], dav[:], -1.0, None, ALU.mult).then_inc(dt_done, 1)

            dv.wait_ge(v_mm, 16)
            for i in range(4, XBC):
                conv(i)
            dv.wait_ge(ds_mm, 1)
            link(V.tensor_copy(dts[:], ps[:, 6, 256:256 + 64].rearrange("p (i b) -> p i b", i=8)))
            tt(eA[:], dts[:], bc(aexp[:], 2, NS), ALU.mult)
            ts(eA[:], eA[:], -1.0, None, ALU.mult)
            dv.wait_ge(silu_done, XBC)
            V.tensor_tensor(xds[:], dts[:], xcX[:, :, NP_:N], ALU.mult).then_inc(ds_ev, 1)

            def sample_c(b):
                dv.wait_ge(hn_done, b + 1)
                tt(smv.rearrange("p (g i) n -> p g i n", g=2), bc(bcb[b][:, 2:4], 2, 4),
                   h0b[b % 2].rearrange("p (g i) n -> p g i n", g=2), ALU.mult)
                V.tensor_reduce(ysm[:, b, :], smv, AX.X, ALU.add).then_inc(smv_done, 1)
                dv.wait_ge(smv_done, b + 1)

            Ug = U[:, 0:G5 * UC].rearrange("p (g c) -> p g c", g=G5)
            dv.wait_ge(lc_mm, 16)
            for c in range(5):
                t0, n = CH[c]
                dv.wait_ge(sa_mm, c + 1)
                link(V.tensor_copy(csv[0:n, 0, :], ps[0:n, 7, 0:16]))
                link(V.tensor_copy(csv[:, 1, :], ps[:, 7, 16:32]))
                link(V.tensor_copy(dev[:, 1, :], csv[:, 1, :]))
                V.tensor_tensor(dev[0:n, 0, :], csv[0:n, 1, :], csv[0:n, 0, :], ALU.subtract).then_inc(de_in, 1)
                tt(cbm[0:n, :, 0:n], ps[0:n, 7, 128:384].rearrange("p (g l) -> p g l", g=2)[:, :, 0:n],
                   bc(tri[0:n, 0:n], 1, 2), ALU.mult)
                for q in range(2):
                    tt(xdt[0:n, 8 * q:8 * q + 8, :], ps[0:n, 4 + q, :].rearrange("p (h d) -> p h d", d=HD),
                       bc(dtv[0:n, c, 8 * q:8 * q + 8], 2, HD), ALU.mult)
                dv.wait_ge(de_out, c + 1)
                V.tensor_tensor(xde[0:n], xdt[0:n], bc(dev[0:n, 0, :], 2, HD), ALU.mult).then_inc(sa_evd, 1)
                if c >= 2:
                    sample_c(2 * c - 4)
                dv.wait_ge(cb_mm, c + 1)
                for h in range(HEADS):
                    last = V.tensor_scalar(Lm[0:n, h, 0:n], ps[0:n, 4 + h // 4, (h % 4) * P:(h % 4) * P + n],
                                           csv[0:n, 0, h:h + 1], 0.0, ALU.subtract, ALU.min)
                    if h % 4 == 3:
                        last.then_inc(l_in, 1)
                if c:
                    dv.wait_ge(e2_done, c + 1)
                    for g in range(2):
                        last = V.tensor_tensor(E2[:, 8 * g:8 * g + 8, 0:n], E2[:, 8 * g:8 * g + 8, 0:n],
                                               bc(xcB[:, 2 + g, t0:t0 + n], 1, 8), ALU.mult)
                    last.then_inc(cs_done, 1)
                dv.wait_ge(l_exp, c + 1)
                for g in range(2):
                    last = V.tensor_tensor(Lm[0:n, 8 * g:8 * g + 8, 0:n], Lm[0:n, 8 * g:8 * g + 8, 0:n],
                                           bc(cbm[0:n, g, 0:n], 1, 8), ALU.mult)
                last.then_inc(m_done, 1)
                if c >= 2:
                    sample_c(2 * c - 3)
                dv.wait_ge(y_mm, c + 1)
                for i in range(8):
                    last = V.scalar_tensor_tensor(ySSD[:, i, t0:t0 + n], xcX[:, i, t0:t0 + n], pf[:, PF_D + i:PF_D + i + 1],
                                                  ps[:, 4 + i // 4, (i % 4) * P:(i % 4) * P + n], ALU.mult, ALU.add)
                last.then_inc(y_ev, 1)
                dv.wait_ge(st_mm, c + 1)
                for g in range(2):
                    hs, pg = Hs[:, 8 * g:8 * g + 8, :], ps[:, 6 + g, :].rearrange("p (h d) -> p h d", d=HD)
                    if c == 0:
                        last = V.tensor_copy(hs, pg)
                    else:
                        tt(hs, hs, bc(dev[:, 1, 8 * g:8 * g + 8], 2, HD), ALU.mult)
                        last = V.tensor_tensor(hs, hs, pg, ALU.add)
                last.then_inc(st_ev, 1)
                if c == 1:
                    for rd in range(16):
                        dv.wait_ge(y5_mm, rd + 1)
                        o = Ug[:, 4 * rd:4 * rd + 4, 0:YC]
                        V.tensor_tensor(o, o, ps[:, 4 + rd % 2, 0:4 * WIN].rearrange("p (q c) -> p q c", q=4)[:, :, 0:YC],
                                        ALU.add).then_inc(y5_ev, 1)
            sample_c(6)
            sample_c(7)
            ys = ySSD[:, :, NP_:N]
            tt(ys, xcX[:, :, NP_:N], bc(pf[:, PF_D:PF_D + 8], 2, NS), ALU.mult)
            tt(ys, ys, ysm[:].rearrange("p b i -> p i b"), ALU.add)
            dv.wait_ge(zs_done, 1)
            dv.wait_ge(y_ev, 5)
            V.tensor_tensor(ySSD, ySSD, zT, ALU.mult).then_inc(gt_done, 1)

            def norm(i, src, gcol):
                dv.wait_ge(ms_done, i + 2)
                root(rmsN, i + 2)
                for k in range(KD):
                    last = V.scalar_tensor_tensor(src[:, k, :], src[:, k, :], pf[:, gcol + k:gcol + k + 1], rmsN,
                                                  ALU.mult, ALU.mult)
                last.then_inc(ys_done, 1)

            for k in range(KD):
                dv.wait_ge(wide_free[k % 2], (28 + k) // 2 + 1)
                V.tensor_tensor(sig[:, k, :], sig[:, k, :], yg[:, k, :], ALU.mult).then_inc(y2_done, 1)
                if k == 3:
                    norm(0, ySSD, PF_GSSD)

            def residual(q):
                for i, (t0, n) in enumerate(TT):
                    o = 5 * q + i
                    dv.wait_ge(o_mm, o + 1)
                    xs_ = x1[i][0:n, 512 * (q % 2):512 * (q % 2) + 512]
                    V.tensor_tensor(xs_, xs_, ps[0:n, o % 4, :], ALU.add).then_inc(o_ev, 1)

            dv.wait_ge(x1_ld, 80)
            residual(0)
            norm(1, sig, PF_GS5)
            for q in range(1, 4):
                residual(q)

            dv.wait_ge(xs_sq, 5)
            V.tensor_scalar(ssum[:], ssum[:], 1.0 / D, EPS, ALU.mult, ALU.add).then_inc(root_in, 1)
            dv.wait_ge(root_out, 4)
            link(V.reciprocal(ssum[:], ssum[:]))
            link(V.memset(lgt, 0.0))
            dv.wait_ge(moe_ld, 48)
            for i, (t0, n) in enumerate(TT):
                if i:
                    dv.wait_ge(x2t_mm, i)
                    dv.wait_ge(x2_st, 16 * i)
                V.scalar_tensor_tensor(x2[0:n, :], x1[i][0:n], ssum[0:n, i:i + 1], gffn[0:n, :],
                                       ALU.mult, ALU.mult).then_inc(x2_done, 1)
            dv.wait_ge(lgt_mm, 5)
            link(V.tensor_copy(lgt[:, 0:4, :], ps[:, 7, 0:144].rearrange("p (i c) -> p i c", i=4)))
            link(V.tensor_copy(lgt[0:24, 4, :], ps[0:24, 7, 144:180]))
            lc = lgt[:, :, 0:EG]
            lf = lgt[:, :, EG:36].rearrange("p i (g e) -> p i g e", g=EG)
            io4, io8 = bc(cst[:, C_IO4:C_IO4 + EG], 1, 5), bc(cst[:, C_IO8:C_IO8 + EPG], 1, 5)

            def first_max(src, m, hot, tmp, iot, w):
                link(V.tensor_reduce(m, src, AX.X, ALU.max))
                tt(tmp, src, bc(m, 2, w), ALU.is_equal)
                ts(tmp, tmp, -99.0, 99.0, ALU.mult, ALU.add)
                tt(tmp, tmp, iot, ALU.add)
                link(V.tensor_reduce(r5, tmp, AX.X, ALU.min))
                tt(hot, iot, bc(r5, 2, w), ALU.is_equal)

            first_max(lc, rm, og, t4, io4, EG)
            V.tensor_tensor(rexp, lc, bc(rm, 2, EG), ALU.subtract).then_inc(r_in, 1)
            t48 = t32.rearrange("p i (g e) -> p i g e", g=EG)
            tt(t48, lf, bc(og, 3, EPG), ALU.mult)
            link(V.tensor_reduce(lsel, t48.rearrange("p i g e -> p i e g"), AX.X, ALU.add))
            first_max(lsel, m1_, o1, t8, io8, EPG)
            stt(lsel, o1, -1e30, lsel, ALU.mult, ALU.add)
            first_max(lsel, m2_, o2, t8, io8, EPG)
            V.tensor_tensor(rdif, m2_, m1_, ALU.subtract).then_inc(r_in, 1)
            val = bc(cst[:, C_VAL:C_VAL + 5], 2, EG)
            tt(og, og, val, ALU.mult)
            for O_, o_ in ((O1, o1), (O2, o2)):
                tt(O_.rearrange("p i (g e) -> p i g e", g=EG), bc(og, 3, EPG), bc(o_, 2, EG), ALU.mult)
            V.tensor_tensor(Ob[:], O1, O2, ALU.add).then_inc(ob_done, 1)
            dv.wait_ge(r_out, 2)
            link(V.tensor_reduce(rm, rexp, AX.X, ALU.add))
            ts(r5, rdif, 1.0, None, ALU.add)
            tt(rm, rm, r5, ALU.mult)
            link(V.reciprocal(gate[:, 0, :], rm))
            tt(gate[:, 1, :], gate[:, 0, :], rdif, ALU.mult)
            dv.wait_ge(rank_mm, 1)
            link(V.tensor_copy(rank, ps[:, 7, 256:256 + 5 * E].rearrange("p (i e) -> p i e", i=5)))
            link(V.tensor_copy(cn[:, 0, :], ps[:, 7, 256 + 5 * E:256 + 6 * E]))
            link(V.memset(cn[:, 1, :], 1.0))
            for k in range(1, -(-N // T)):
                stt(cn[:, 1, :], cn[:, 0, :], float(T * k), cn[:, 1, :], ALU.is_gt, ALU.add)
            link(V.memset(cn[:, 2, :], 0.0))
            link(V.tensor_copy(cn[:, 2, 1:E], cn[:, 1, 0:E - 1]))
            src_, dst_ = 2, 0
            sh = 1
            while sh < E:
                link(V.tensor_copy(cn[:, dst_, 0:sh], cn[:, src_, 0:sh]))
                tt(cn[:, dst_, sh:E], cn[:, src_, sh:E], cn[:, src_, 0:E - sh], ALU.add)
                src_, dst_ = dst_, src_
                sh *= 2
            ahead = cn[:, src_, :]
            link(V.tensor_copy(cum[0:1, 0:E], ahead[0:1, :]))
            tt(cum[0:1, E:E + 1], ahead[0:1, E - 1:E], cn[0:1, 1, E - 1:E], ALU.add)
            stt(rank, bc(ahead, 1, 5), float(T), rank, ALU.mult, ALU.add)
            for k, O_ in enumerate((O1, O2)):
                tt(t32, O_, rank, ALU.mult)
                link(V.tensor_reduce(r5, t32, AX.X, ALU.add))
                link(V.tensor_copy(slot[:, :, k], r5))
                ts(rm, r5, 1.0 / T, (T - 1) / (2 * T), ALU.mult, ALU.subtract)
                ts(rm, rm, MAGIC, MAGIC, ALU.add, ALU.subtract)
                ts(r5, r5, float(IDXC), None, ALU.mult)
                stt(r5, rm, float(1 - T * IDXC), r5, ALU.mult, ALU.add)
                last = V.tensor_copy(place[:, :, k], r5)
                if k == 0:
                    link(last)
            last.then_inc(slot_done, 1)

            dv.wait_ge(slot_done, 1)
            nt = tile_bound(dv, slice(E, E + 1), E)
            dv.sem_inc(hr, 1)
            dv.wait_ge(xtr, 2)
            V.tensor_copy(xtf, ps[:, 2, :]).then_inc(xev, 1)
            with dv.Fori(0, nt) as q:
                dv.wait_ge(silu, q + 2)
                dv.wait_ge(umm, q + 1)
                dv.wait_ge(htr, q + 1)
                V.tensor_tensor(hh, sg, ps[:, 1, 0:256], ALU.mult).then_inc(hr, 1)
                dv.wait_ge(xtr, q + 3)
                V.tensor_copy(xtf, ps[:, 2, :]).then_inc(xev, 1)
                dv.wait_ge(htr, q + 2)
                dv.wait_ge(dmm, q + 1)
                V.tensor_copy(ht.rearrange("p a b -> p (a b)"), ps[:, 3, 0:256]).then_inc(hev, 1)
            for i, (t0, n) in enumerate(TT):
                dv.wait_ge(gy[i], 32)
                xs_ = x1[i][0:n]
                stt(xs_, G[2 * i][0:n], gate[0:n, 0, i:i + 1], xs_, ALU.mult, ALU.add)
                V.scalar_tensor_tensor(xs_, G[2 * i + 1][0:n], gate[0:n, 1, i:i + 1], xs_,
                                       ALU.mult, ALU.add).then_inc(fin_done, 1)
            dv.wait_ge(xs_sq, 10)
            V.tensor_scalar(ssum[:], ssum[:], 1.0 / D, EPS, ALU.mult, ALU.add).then_inc(root_in, 1)
            dv.wait_ge(root_out, 5)
            link(V.reciprocal(ssum[:], ssum[:]))
            for i, (t0, n) in enumerate(TT):
                xs_ = x1[i][0:n]
                V.scalar_tensor_tensor(xs_, xs_, ssum[0:n, i:i + 1], gfin[0:n, :], ALU.mult, ALU.mult).then_inc(fo_done, 1)


def kernel(**inputs):
    import concourse.bacc as bacc
    from concourse.bass_utils import run_bass_kernel_spmd as run

    x = {k: np.asarray(v) for k, v in inputs.items()}
    f32 = np.float32
    toks = np.concatenate([x["meta_tokens"], x["x_prompt"][0], x["x_sample"][:, 0]], 0)

    def feat(v):
        v = v.reshape(v.shape[0] // P, P, -1)
        return np.ascontiguousarray(v.transpose(1, 0, 2)).reshape(P, -1)

    def tiles(w):
        w = w.reshape(KD, P, w.shape[1] // P, P)
        return np.ascontiguousarray(w.transpose(2, 1, 0, 3)).reshape(w.shape[2], P, KD * P)

    w_in = x["w_in"][0]
    c_z, c_x, c_b, c_dt, c_u = 0, D, 2 * D, D + 1536, D + 1536 + HEADS
    wi = tiles(np.concatenate([w_in[:, c_u:], w_in[:, c_b:c_dt], w_in[:, c_x:c_b], w_in[:, c_z:c_x]], 1))
    t = lambda v: v.T
    pf = np.concatenate([
        feat(x["norm_mix"][0]), feat(t(x["conv_w"][0])), feat(x["conv_b"][0]), feat(np.repeat(x["d_ssd"][0], HD)),
        feat(x["ssd_norm"][0]), feat(x["s5_norm"][0]), feat(x["b_glu"][0]), feat(np.repeat(x["a_log"][0], HD))], 1)
    two = lambda u, v: np.concatenate([u, v], 0)
    are, aim = t(x["s5_a_re"][0]), t(x["s5_a_im"][0])
    s5p = np.concatenate([two(are, are), two(aim, aim), np.broadcast_to(x["s5_log_dt"][0], (P, G5))], 1)
    cr, ci = (x[k][0].transpose(2, 0, 1).reshape(S5, -1) for k in ("s5_c_re", "s5_c_im"))
    br, bi = (x[k][0].transpose(1, 0, 2).reshape(S5, -1) for k in ("s5_b_re", "s5_b_im"))
    s5stk = np.concatenate([two(cr, ci), two(ci, cr), two(br, bi), two(bi, br)], 1)
    s5bt = np.stack([x["s5_b_re"][0], x["s5_b_im"][0]]).transpose(3, 1, 0, 2).reshape(C5, -1)
    dk = np.zeros((4, 32, 16), f32)
    dk[:, :C5] = x["s5_d"][0].reshape(16, 4, C5).transpose(1, 2, 0)
    cst_in = x["state_ssd_conv"][0].reshape(NS, 3, XBC, P).transpose(3, 1, 2, 0).reshape(P, -1)
    h0s5 = np.stack([x["state_s5_re"][0], x["state_s5_im"][0]]).transpose(0, 3, 1, 2)
    wrt = np.concatenate([x["router_coarse_w"][0], x["router_fine_w"][0].transpose(1, 0, 2).reshape(D, E)], 1)
    br_ = np.concatenate([x["router_coarse_b"][0], x["router_fine_b"][0].reshape(-1)])[:, None]
    i = np.arange(P)
    cs = np.zeros((P, C_N), f32)
    cs[:, C_ID:C_ID + P] = np.eye(P)
    cs[:, C_TRI:C_TRI + P] = i[:, None] <= i[None]
    cs[:, C_SGN], cs[:, C_M0], cs[:, C_M1] = np.where(i < 64, 1, -1), i < 64, i >= 64
    cs[:, C_IO8:C_IO8 + EPG], cs[:, C_IO4:C_IO4 + EG] = np.arange(EPG), np.arange(EG)
    cs[:, C_VAL:C_VAL + 5] = i[:, None] + P * np.arange(5) < N
    onb = np.concatenate([np.ones((P, P)), i[:, None] < i[None]], 1).astype(mybir.dt.np(BF16))

    ins = {
        "consts": cs, "onb": onb, "pf": pf, "xT": feat(t(toks)), "xtok": toks, "wi": wi, "wglu": tiles(x["w_glu"][0]),
        "wdt": feat(w_in[:, c_dt:c_u]), "dtb": x["dt_bias"][0][:, None], "alog": x["a_log"][0],
        "s5p": s5p, "s5stk": s5stk, "s5bt": s5bt, "s5dk": dk.reshape(P, 16), "h0s5": h0s5.reshape(2, S5, NS * G5),
        "cst_in": cst_in, "ssm_in": x["state_ssd_ssm"][0].reshape(NS, HEADS * HD, NSTATE),
        "w_out": x["w_out"][0], "wr": feat(wrt), "br": br_, "gffn": x["norm_ffn"][0], "gfin": x["norm_final"],
        "w_gate": x["w_gate"][0], "w_up": x["w_up"][0], "w_down": x["w_down"][0],
    }
    ins = {k: np.ascontiguousarray(v) for k, v in ins.items()}
    outs = {
        "o_y": (N, D), "o_conv_p": (P, XBC * 3), "o_conv_s": (P, XBC * NS * 3), "o_ssm_p": (P, HEADS * HD),
        "o_ssm_s": (NS, HEADS * HD, NSTATE), "o_s5p": (2, S5, G5), "o_s5s": (2, S5, NS * G5),
    }
    nc = bacc.Bacc("TRN2", target_bir_lowering=False, num_devices=1)
    a = {k: nc.dram_tensor(k, v.shape, mybir.dt.from_np(v.dtype), kind="ExternalInput").ap() for k, v in ins.items()}
    a |= {k: nc.dram_tensor(k, s, F32, kind="ExternalOutput").ap() for k, s in outs.items()}
    build(nc, a)
    r = run(nc, [ins], core_ids=[0]).results[0]
    y = r["o_y"]
    unfeat = lambda v, *s: v.reshape(P, XBC, -1).transpose(2, 1, 0).reshape(*s)
    s5p_o, s5s_o = r["o_s5p"], r["o_s5s"].reshape(2, S5, NS, G5)
    res = (
        y[META:NP_][None], y[NP_:][:, None],
        unfeat(r["o_conv_p"], 1, 1, 3, XBC * P),
        r["o_ssm_p"].T.reshape(1, 1, HEADS, HD, NSTATE),
        s5p_o[0].T[None, None], s5p_o[1].T[None, None],
        r["o_conv_s"].reshape(P, 3, XBC, NS).transpose(3, 1, 2, 0).reshape(1, NS, 3, XBC * P),
        r["o_ssm_s"].reshape(1, NS, HEADS, HD, NSTATE),
        s5s_o[0].transpose(1, 2, 0)[None], s5s_o[1].transpose(1, 2, 0)[None],
    )
    return tuple(np.ascontiguousarray(v) for v in res)
```

```python
from contextlib import ExitStack

import numpy as np
import concourse.bass as bass
from concourse import mybir

F32 = mybir.dt.float32
F32R = mybir.dt.float32r
BF16 = mybir.dt.bfloat16
I32 = mybir.dt.int32
ACT = mybir.ActivationFunctionType
ALU = mybir.AluOpType
AX = mybir.AxisListType

P = 128
D = 1024
KD = D // P
SEQ = 512
META = 16
NP_ = META + SEQ
NS = 8
N = NP_ + NS
SPLIT = 264
HALVES = ((0, SPLIT), (SPLIT, N))
TT = [(i * P, min(P, N - i * P)) for i in range(5)]
CH = [(i * P, min(P, NP_ - i * P)) for i in range(5)]
EPS = 1e-6

HEADS, HD, NSTATE, CONV = 16, 64, 128, 4
XBC = 12

G5, C5, S5 = 64, 16, 64
J = 8
NC5 = NP_ // J
COL_S0 = NC5 + 1
COL_S7 = COL_S0 + NS
UC = COL_S7 + NS
WIN = 96
YC = COL_S7

E, EPG, EG, FF = 32, 8, 4, 512
T = 64
MAXT = E + (2 * N) // (T + 1)
IDXC = 56
RING = 4
WBUF = 3
E_LOOP = E // WBUF

PF_GMIX, PF_CW, PF_CB, PF_D, PF_GSSD, PF_GS5, PF_BGLU, PF_ALOG, PF_N = 0, 8, 56, 68, 76, 84, 92, 100, 108
C_ID, C_TRI, C_SGN, C_M0, C_M1, C_VAL, C_TOK, C_IO, C_N = 0, 128, 256, 257, 258, 259, 264, 269, 333

MAGIC = 12582912.0
TWO_PI_HI, TWO_PI_MID = 6.28125, 0.0019340515136718750
TWO_PI_LO = 2 * np.pi - TWO_PI_HI - TWO_PI_MID
PI_F = 3.1415925


def build(nc, a):
    ctx = ExitStack()
    with ctx:
        def sb(name, shape, dt=F32):
            return ctx.enter_context(nc.sbuf_tensor("sb_" + name, shape, dt))

        def sem(name):
            return ctx.enter_context(nc.semaphore(name))

        def scratch(name, shape, dt=F32):
            return nc.dram_tensor(name, shape, dt, kind="Internal").ap()

        u_scr = scratch("u_scr", [D, N])
        q_scr = scratch("q_scr", [J, G5 * 2 * S5])
        y_scr = scratch("y_scr", [D, N])
        x2_scr = scratch("x2_scr", [N, D])
        ye_scr = scratch("ye_scr", [(MAXT + RING) * T, D])

        arena_at = -(-nc.sbuf_base // 32) * 32
        arena = sb("arena", [P, 47408])

        def rounded(name, off, *shape):
            return nc.alloc_sbuf_tensor_at("sb_" + name, [P, *shape], F32R, offset=arena_at + 4 * off)

        def part(off, *shape, p=(0, P)):
            n = int(np.prod(shape))
            v = arena[p[0]:p[1], off:off + n]
            if len(shape) == 1:
                return v
            names = "abcd"[:len(shape)]
            return v.rearrange(f"p ({' '.join(names)}) -> p {' '.join(names)}",
                               **{k: s for k, s in zip(names, shape)})

        xn = part(0, KD, N)
        ring = [part(4288 + 1024 * i, KD, P) for i in range(3)]
        raw = [part(7360 + 576 * i, 576) for i in range(2)]
        xcB = part(8512, 4, N)
        xcX = part(10656, 8, N)
        uD = [part(10656 + N * i, N) for i in range(2)]
        Vm = part(10656, 32, 2, S5)
        dt_raw = part(34864, N, p=(0, HEADS))
        sp_u, sp_s, sp_z = (part(35400 + 80 * i, 80) for i in range(3))
        wdt = part(14752, KD, HEADS)
        U = part(14944, 5328)
        Wp = part(20272, G5, J + 1, C5)
        HA_off = 29488
        xT = part(29488, KD, N)
        sq0 = part(33776, KD, N)
        Wt = part(29488, G5, J + 1, C5)
        rms0 = part(20272, N)
        pw_t = part(33776, 4 * G5)
        smp = part(34352, NS, G5)
        dkt = part(38704, 16, C5)
        stk = part(39216, 4, G5, C5)
        QB = part(39216, 32, 2, S5)
        BT = part(43312, 32, 2, S5)
        Tm = part(39216, G5, J, C5)
        Bb = part(39216 + 2048, (G5 + 1) * C5)
        tmp = 43312

        def tv(i):
            return part(tmp + G5 * i, G5)

        Pre, Pim = part(tmp + 1280, J + 1, G5), part(tmp + 1856, J + 1, G5)
        Qs, qt = part(tmp + 2432, J, G5), part(tmp + 2944, 4, P)
        zT = part(35632, 8, N)
        Lm = part(39920, HEADS, P)
        E2 = part(41968, HEADS, P)
        xdt = part(44016, HEADS, HD)
        xde = part(45040, HEADS, HD)
        cbm = part(46064, 2, P)
        btok = part(46320, 2, P)
        ySSD = xcX
        bts = part(20352, 4, NSTATE)
        h0b = [part(20864 + 1024 * i, 8, NSTATE) for i in range(2)]
        smt, smu, smv = (part(22912 + 1024 * i, 8, NSTATE) for i in range(3))
        bcb = [part(25984 + 512 * i, 4, NSTATE) for i in range(NS)]
        yraw = part(14944, 8, N)
        yg = part(0, KD, N)
        sig = part(30832, KD, N)
        sq = part(39920, KD, N)
        wo = [part(14944, KD, 512), part(4288, KD, 512)]
        wo_hi, wo_lo, y_hi, y_lo = (
            [rounded(f"{name}{i}", off, KD, w) for i, off in enumerate(offs)] for name, w, offs in (
                ("wo_hi", 512, (26736, 35120)), ("wo_lo", 512, (14944, 4288)),
                ("y_hi", N, (22448, 39920)), ("y_lo", N, (10656, 30832))))
        W_off = [35120, 22640, 10352]
        Wg = [part(o, KD, FF) for o in W_off]
        Wu = [part(o + 4096, KD, FF) for o in W_off]
        Wd = [part(o + 8192, 4, D) for o in W_off]
        xg = [part(4288 + 1024 * i, D, p=(0, T)) for i in range(RING)]
        oh_row, oh_tile = part(4288, 10, T), part(4928, 10, IDXC)
        xst = part(8384, D, p=(0, T))
        xt = part(9408, KD, T)
        xtf = part(9408, KD * T)
        ht = part(9920, 2, P)
        gffn = part(8512, D)
        wr = part(9664, KD, 36)
        x2 = part(18544, D)
        x2T = part(19568, KD, P)
        lgs = part(20592, P, p=(0, 36))
        junk = arena[:, 20720:21232].bitcast(BF16)
        rt = [21232]

        def small(*shape):
            rt[0] += int(np.prod(shape))
            return part(rt[0] - int(np.prod(shape)), *shape)

        lgt, rexp, og, t4 = small(5, 36), small(5, EG), small(5, EG), small(5, EG)
        o1, o2, t8, lsel = (small(5, EPG) for _ in range(4))
        t32, O1, O2, rank, cn = small(5, E), small(5, E), small(5, E), small(5, E), small(3, E)
        slf, stf = small(5, 2), small(5, 2)
        Ob = small(5 * E // 2).bitcast(BF16).rearrange("p (i e) -> p i e", e=E)
        rm, r5, m1_, m2_, rdif = (small(5) for _ in range(5))
        assert rt[0] <= 22640
        G = [part(10352 + 1024 * i, D) for i in range(10)]
        gfin = part(20592, D)

        cst = sb("cst", [P, C_N])
        pf = sb("pf", [P, PF_N])
        ones = sb("ones", [P, P])
        kxf = sb("kxf", [P, 2048 + 1024])
        Kx = kxf[:, 0:2048].rearrange("p (a j c) -> p a j c", a=16, j=J)
        dK = sb("dK", [P, 16])
        Hs = kxf[:, 0:D].rearrange("p (h d) -> p h d", d=HD)
        x1 = [part(1024 * i, D) for i in range(4)] + [kxf[:, 0:D]]
        rmsN = kxf[:, D:D + N]
        yo = [kxf[:, D + 512 * u:D + 512 * u + 512] for u in range(RING)]
        Aj = sb("Aj", [P, 2, 2, G5])
        sst = sb("sst", [P, NS, G5])
        rec = sb("rec", [P, 2, G5])
        sg, hh = (sst[:].rearrange("p b g -> p (b g)")[:, 256 * i:256 * i + 256] for i in range(2))
        ncp = sb("ncp", [P, XBC, CONV - 1])
        ncs = sb("ncs", [P, XBC, NS])
        scv = sb("scv", [P, CONV - 1, XBC, NS])
        dtb = sb("dtb", [HEADS, 1])
        arow = sb("arow", [P, HEADS])
        dtv = sb("dtv", [P, 5, HEADS])
        dav = sb("dav", [P, 5, HEADS])
        csv = sb("csv", [P, 2, HEADS])
        dev = sb("dev", [P, 2, HEADS])
        aexp = sb("aexp", [P, 8])
        eA = sb("eA", [P, 8, NS])
        dts = sb("dts", [P, 8, NS])
        xds = sb("xds", [P, 8, NS])
        ysm = sb("ysm", [P, NS, 8])
        ssum = sb("ssum", [P, 5])
        idx = sb("idx", [T, IDXC], I32)
        idc = [sb(f"idc{i}", [T, 1], I32)[:] for i in range(RING)]
        cum = sb("cum", [1, E + 1], I32)
        slot = sb("slot", [P, 5, 2], I32)
        gate = sb("gate", [P, 2, 5])
        brc = sb("brc", [36, 1])
        onb = sb("onb", [P, 2, P], BF16)

        ps = ctx.enter_context(nc.psum_tensor("ps", [P, 8, 512], F32))
        ident = cst[:, C_ID:C_ID + P]
        tri = cst[:, C_TRI:C_TRI + P]

        def bc(ap, axis, n):
            v = ap.unsqueeze(axis)
            return v.broadcast_to([*v.shape[:axis], n, *v.shape[axis + 1:]])

        ld_x = [sem(f"ld_x{i}") for i in range(2)]
        ld_const, ld_s5, ld_stk, ld_misc = sem("ld_const"), sem("ld_s5"), sem("ld_stk"), sem("ld_misc")
        ring_full = [sem(f"ring_full{i}") for i in range(3)]
        wide_done = sem("wide_done")
        wide_free = [sem(f"wide_free{i}") for i in range(2)]
        ones_set, sq_done, ms_done, root_in, root_out = (sem(x) for x in (
            "ones_set", "sq_done", "ms_done", "root_in", "root_out"))
        xn_done = sem("xn_done")
        dve, pool, act = sem("dve_order"), sem("pool_order"), sem("act_order")
        s5_act, s5_dve = sem("s5_act"), sem("s5_dve")
        pow_done, wt_done, wp_done, sqt_done, q_done = (sem(x) for x in (
            "pow_done", "wt_done", "wp_done", "sqt_done", "q_done"))
        k_mm, k_ev, qt_mm, qt_ev, q_st = (sem(x) for x in ("k_mm", "k_ev", "qt_mm", "qt_ev", "q_st"))
        u_st = [sem(f"u_st{i}") for i in range(2)]
        u_ld, u_zero, t_zero, t_ld, h0_ld = (sem(x) for x in (
            "u_ld", "u_zero", "t_zero", "t_ld", "h0_ld"))
        qb_ld = [sem(f"qb_ld{i}") for i in range(2)]
        v_done, v_mm, v_ev = sem("v_done"), sem("v_mm"), sem("v_ev")
        lc_mm, lc_ev = sem("lc_mm"), sem("lc_ev")
        raw_done, conv_done, silu_done = sem("raw_done"), sem("conv_done"), sem("silu_done")
        h_done, y5_mm, y5_ev, y5_st = sem("h_done"), sem("y5_mm"), sem("y5_ev"), sem("y5_st")
        outs = sem("outs")
        s5_out = sem("s5_out")
        dt_mm, dt_ev, dtt_mm, dt_done = sem("dt_mm"), sem("dt_ev"), sem("dtt_mm"), sem("dt_done")
        sa_mm, sa_evd, sa_eva, de_in, de_out = (sem(x) for x in ("sa_mm", "sa_evd", "sa_eva", "de_in", "de_out"))
        cb_mm, l_in, l_exp, e2_done, m_done, cs_done = (sem(x) for x in (
            "cb_mm", "l_in", "l_exp", "e2_done", "m_done", "cs_done"))
        y_mm, y_ev, st_mm, st_ev, ssm_out = (sem(x) for x in (
            "y_mm", "y_ev", "st_mm", "st_ev", "ssm_out"))
        ds_mm, ds_ev, ea_out, bcs_mm, bcs_ev = (sem(x) for x in ("ds_mm", "ds_ev", "ea_out", "bcs_mm", "bcs_ev"))
        h0s_ld = [sem(f"h0s_ld{i}") for i in range(2)]
        h0s_st = [sem(f"h0s_st{i}") for i in range(2)]
        hn_done = sem("hn_done")
        zs_done, gt_done, ys_done = sem("zs_done"), sem("gt_done"), sem("ys_done")
        yraw_ld, smv_done = sem("yraw_ld"), sem("smv_done")
        gelu_done, y2_done = sem("gelu_done"), sem("y2_done")
        wo_ld = [sem(f"wo_ld{i}") for i in range(2)]
        wo_hid, wo_lod, yn_done, yh_done = sem("wo_hid"), sem("wo_lod"), sem("yn_done"), sem("yh_done")
        x1_ld, o_mm, o_ev = sem("x1_ld"), sem("o_mm"), sem("o_ev")
        moe_ld, xs_sq, x2_done, x2_st, x2t_mm, x2t_ev, lg_mm, lg_ev, lgt_mm = (
            sem(x) for x in ("moe_ld", "xs_sq", "x2_done", "x2_st", "x2t_mm",
                             "x2t_ev", "lg_mm", "lg_ev", "lgt_mm"))
        r_in, r_out, ob_done, rank_mm, slot_done, oh_done, tab_mm, tab_ev = (sem(x) for x in (
            "r_in", "r_out", "ob_done", "rank_mm", "slot_done", "oh_done", "tab_mm", "tab_ev"))
        wg_ld = [sem(f"wg_ld{i}") for i in range(WBUF)]
        wu_ld = [sem(f"wu_ld{i}") for i in range(WBUF)]
        wd_ld = [sem(f"wd_ld{i}") for i in range(WBUF)]
        gath = [sem(f"gath{i}") for i in range(RING)]
        idc_done, staged, xtr, xev, gmm, umm, silu, hr, htr, hev, dmm, yev = (sem(x) for x in (
            "idc_done", "staged", "xtr", "xev", "gmm", "umm", "silu", "hr", "htr", "hev", "dmm", "yev"))
        yst = [sem(f"yst{i}") for i in range(RING)]
        gy = [sem(f"gy{i}") for i in range(5)]
        fin_done, fo_done, ye_zero = sem("fin_done"), sem("fo_done"), sem("ye_zero")

        gsrc = a["w_gate"].rearrange("e (p k) n -> e p k n", k=KD)
        usrc = a["w_up"].rearrange("e (p k) n -> e p k n", k=KD)
        dsrc = a["w_down"].rearrange("e (k p) n -> e p k n", k=4)

        def conv_tile(i):
            return 8 + i if i < 4 else i - 4

        def conv_dst(i):
            return xcB[:, i, :] if i < 4 else xcX[:, i - 4, :]

        NW = 36

        def tile_bound(eng, i, least):
            return eng.value_load(cum[0:1, i], min_val=least, max_val=MAXT)

        block = ctx.enter_context(nc.Block())


        @block.sync
        def _(sp):
            sp.dma_start(cst[:], a["consts"]).then_inc(ld_const, 16)
            sp.dma_start(pf[:], a["pf"]).then_inc(ld_const, 16)
            for i in range(2):
                sp.dma_start(xT[:, 4 * i:4 * i + 4, :],
                             a["xT"].rearrange("p (k n) -> p k n", k=KD)[:, 4 * i:4 * i + 4, :]).then_inc(ld_x[i], 16)
            sp.dma_start(part(tmp, 3, G5), a["s5p"].rearrange("p (a g) -> p a g", a=3)).then_inc(ld_s5, 16)
            for s in range(3):
                sp.dma_start(ring[s], a["wi"][s].rearrange("p (k n) -> p k n", k=KD)).then_inc(ring_full[s], 16)
            sp.dma_start(stk, a["s5stk"].rearrange("p (a g c) -> p a g c", a=4, g=G5)).then_inc(ld_stk, 16)
            sp.dma_start(dK[:], a["s5dk"]).then_inc(ld_misc, 16)
            sp.dma_start(scv[:], a["cst_in"].rearrange("p (j k b) -> p j k b", k=XBC, b=NS)).then_inc(ld_misc, 16)
            sp.dma_start(wdt[:], a["wdt"].rearrange("p (k n) -> p k n", k=KD)).then_inc(ld_misc, 16)
            sp.dma_start(dtb[:], a["dtb"]).then_inc(ld_misc, 16)
            sp.dma_start(arow[:], a["alog"].partition_broadcast(P)).then_inc(ld_misc, 16)
            sp.dma_start(brc[:], a["br"]).then_inc(ld_misc, 16)
            sp.dma_start(onb[:], a["onb"].rearrange("p (a q) -> p a q", a=2)).then_inc(ld_misc, 16)
            sp.dma_start(a["o_conv_s"][:, 0:2 * XBC * NS], a["cst_in"][:, XBC * NS:3 * XBC * NS]).then_inc(outs, 16)

            def ring_load(w):
                sp.wait_ge(wide_done, w - 2)
                src = a["wi"][w] if w < 28 else a["wglu"][w - 28]
                sp.dma_start(ring[w % 3], src.rearrange("p (k n) -> p k n", k=KD)).then_inc(ring_full[w % 3], 16)

            for w in (3, 4):
                ring_load(w)
            sp.wait_ge(u_zero, 1)
            for i in range((MAXT - E) * T // P // 4):
                sp.dma_start(ye_scr[E * T + 4 * P * i:E * T + 4 * P * (i + 1), :].rearrange("(p n) d -> p (n d)", p=P),
                             U[:, 0:4 * D]).then_inc(ye_zero, 16)
            for w in (5, 6, 7):
                ring_load(w)
            sp.wait_ge(qt_ev, 1)
            qdst = q_scr.rearrange("(b j) (g r) -> j g b r", j=2, g=G5)
            for j in range(2):
                sp.dma_start(qdst[j], qt[64 * j:64 * j + 64]).then_inc(q_st, 16)
            for w in (8, 9):
                ring_load(w)
            for s in range(2):
                sp.wait_ge(u_st[s], 64)
            sp.wait_ge(ye_zero, 32)
            Ug = U[:, 0:G5 * UC].rearrange("p (g c) -> p g c", g=G5)
            usrc5 = u_scr[:, 0:NP_].rearrange("(g c) (j m) -> j c g m", c=C5, j=J)
            us5 = u_scr[:, NP_:N].rearrange("(g c) b -> c g b", c=C5)
            for j in range(J):
                sp.dma_start(Ug[16 * j:16 * j + 16, :, 0:NC5], usrc5[j]).then_inc(u_ld, 16)
            sp.dma_start(Ug[0:16, :, COL_S0:COL_S0 + NS], us5).then_inc(u_ld, 16)
            sp.dma_start(Ug[16 * (J - 1):16 * J, :, COL_S7:COL_S7 + NS], us5).then_inc(u_ld, 16)
            for w in (10, 11):
                ring_load(w)

            def qb_loads(half):
                for j in range(J):
                    sp.dma_start(QB[16 * j:16 * j + 16],
                                 q_scr[j, 4096 * half:4096 * half + 4096].partition_broadcast(16)
                                 .rearrange("q (g r s) -> q g r s", g=32, r=2)).then_inc(qb_ld[half], 16)
                    sp.dma_start(BT[16 * j:16 * j + 16],
                                 a["s5bt"][:, 4096 * half:4096 * half + 4096]
                                 .rearrange("q (g r s) -> q g r s", g=32, r=2)).then_inc(qb_ld[half], 16)

            sp.wait_ge(q_st, 32)
            sp.wait_ge(k_mm, 1)
            qb_loads(0)
            for w in (12, 13):
                ring_load(w)
            sp.wait_ge(v_done, 1)
            qb_loads(1)
            for w in (14, 15):
                ring_load(w)

            def toeplitz(r):
                for j in range(J):
                    sp.dma_start(Tm[16 * j:16 * j + 16, r::4, j:J, :],
                                 Kx[32 * r:32 * r + 16, :, 0:J - j, :]).then_inc(t_ld, 16)

            sp.wait_ge(t_zero, 1)
            sp.wait_ge(k_ev, 2)
            toeplitz(0)
            toeplitz(1)
            ring_load(16)
            toeplitz(2)
            toeplitz(3)
            for w in range(17, 22):
                ring_load(w)
            sp.wait_ge(conv_done, XBC)
            sp.dma_start(a["o_conv_p"].rearrange("p (k j) -> p k j", k=XBC), ncp[:]).then_inc(outs, 16)
            sp.dma_start(a["o_conv_s"][:, 2 * XBC * NS:], ncs[:].rearrange("p k b -> p (k b)")).then_inc(outs, 16)
            for w in range(22, 26):
                ring_load(w)
            sp.wait_ge(y5_ev, 16)
            ydst = y_scr[:, 0:NP_].rearrange("(g c) (j m) -> j c g m", c=C5, j=J)
            for j in range(J):
                sp.dma_start(ydst[j], Ug[16 * j:16 * j + 16, :, 0:NC5]).then_inc(y5_st, 16)
            sp.dma_start(y_scr[:, NP_:N].rearrange("(g c) b -> c g b", c=C5),
                         Ug[0:16, :, COL_S0:COL_S0 + NS]).then_inc(y5_st, 16)
            ring_load(26)
            sp.wait_ge(y5_st, 16 * 9)
            sp.dma_start(yraw, y_scr.rearrange("(k p) n -> p k n", p=P)).then_inc(yraw_ld, 16)
            for w in range(27, 31):
                ring_load(w)
            wsrc = a["w_out"].rearrange("(k p) n -> p k n", p=P)

            def wo_load(q):
                sp.dma_start(wo[q % 2], wsrc[:, 8 * (q // 2):8 * (q // 2) + 8,
                                             512 * (q % 2):512 * (q % 2) + 512]).then_inc(wo_ld[q % 2], 16)

            sp.wait_ge(gelu_done, 8)
            wo_load(0)
            sp.wait_ge(st_ev, 5)
            sp.dma_start(a["o_ssm_p"], Hs.rearrange("p h d -> p (h d)")).then_inc(ssm_out, 16)
            for w in range(31, NW):
                ring_load(w)
            sp.wait_ge(y2_done, 8)
            sp.wait_ge(ssm_out, 16)
            for i, (t0, n) in enumerate(TT):
                sp.dma_start(x1[i][0:n], a["xtok"][t0:t0 + n, :]).then_inc(x1_ld, 16)
            sp.wait_ge(wide_done, NW)
            wo_load(1)
            sp.wait_ge(gt_done, 1)
            sp.dma_start(gffn, a["gffn"].partition_broadcast(P)).then_inc(moe_ld, 16)
            sp.dma_start(wr, a["wr"].rearrange("p (k n) -> p k n", k=KD)).then_inc(moe_ld, 16)
            sp.wait_ge(o_mm, 5)
            wo_load(2)
            sp.wait_ge(o_mm, 10)
            wo_load(3)
            sp.dma_start(Wg[1], gsrc[1]).then_inc(wg_ld[1], 16)
            sp.dma_start(Wg[2], gsrc[2]).then_inc(wg_ld[2], 16)
            sp.wait_ge(o_mm, 15)
            sp.dma_start(Wu[1], usrc[1]).then_inc(wu_ld[1], 16)
            sp.dma_start(Wu[2], usrc[2]).then_inc(wu_ld[2], 16)
            sp.wait_ge(o_mm, 20)
            sp.dma_start(Wg[0], gsrc[0]).then_inc(wg_ld[0], 16)
            sp.dma_start(Wu[0], usrc[0]).then_inc(wu_ld[0], 16)
            sp.dma_start(Wd[0], dsrc[0]).then_inc(wd_ld[0], 16)
            sp.dma_start(Wd[1], dsrc[1]).then_inc(wd_ld[1], 16)
            sp.wait_ge(tab_ev, 1)
            sp.wait_ge(gath[RING - 1], 16)
            sp.dma_start(Wd[2], dsrc[2]).then_inc(wd_ld[2], 16)

            def load_expert(s, gate_src, up_src, down_src, before):
                done = tile_bound(sp, before, 1)
                sp.wait_ge(umm, done)
                sp.dma_start(Wg[s], gate_src).then_inc(wg_ld[s], 16)
                sp.dma_start(Wu[s], up_src).then_inc(wu_ld[s], 16)
                sp.wait_ge(dmm, done + 1)
                sp.dma_start(Wd[s], down_src).then_inc(wd_ld[s], 16)

            with sp.Fori(1, E_LOOP) as ep:
                for s in range(WBUF):
                    e = ep * WBUF + s
                    load_expert(s, *(w[bass.ds(e, 1)].rearrange("a p k n -> (a p) k n") for w in (gsrc, usrc, dsrc)),
                                bass.ds(e - (WBUF - 1), 1))
            for e in range(E_LOOP * WBUF, E):
                load_expert(e % WBUF, gsrc[e], usrc[e], dsrc[e], slice(e - WBUF + 1, e - WBUF + 2))
            done = tile_bound(sp, slice(E_LOOP * WBUF, E_LOOP * WBUF + 1), 1)
            sp.wait_ge(dmm, done + 1)
            sp.dma_start(gfin, a["gfin"].partition_broadcast(P)).then_inc(moe_ld, 16)
            for i, (t0, n) in enumerate(TT):
                sp.wait_ge(fo_done, i + 1)
                sp.dma_start(a["o_y"][t0:t0 + n, :], x1[i][0:n]).then_inc(outs, 16)
            for s in range(2):
                sp.wait_ge(h0s_st[s], 64)
            sp.wait_ge(s5_out, 32)
            sp.wait_ge(ssm_out, 16)
            sp.wait_ge(outs, 16 * 8)

        @block.gpsimd
        def _(pl):
            cnt = [0]

            def link(ins):
                cnt[0] += 1
                ins.then_inc(pool, 1)
                pl.wait_ge(pool, cnt[0])

            nc.gpsimd.memset(U, 0.0).then_inc(u_zero, 1)
            pl.wait_ge(ld_stk, 16)
            pl.wait_ge(pow_done, 1)
            nc.gpsimd.tensor_tensor(Wt, bc(stk[:, 1], 2, J + 1), bc(Pim.rearrange("p t g -> p g t"), 3, C5),
                                    ALU.mult).then_inc(wt_done, 1)
            pl.wait_ge(wp_done, 1)
            HA = part(HA_off, 76, G5)
            nc.gpsimd.memset(HA[:, 75], 0.0)
            link(nc.gpsimd.memset(HA[:, 0], 0.0))
            pl.dma_start(HA[:, COL_S0:COL_S0 + NS].rearrange("p b g -> p (b g)"),
                         a["h0s5"].rearrange("r s b -> (r s) b")).then_inc(h0_ld, 16)
            pl.wait_ge(v_done, 2)
            nc.gpsimd.memset(Tm, 0.0).then_inc(t_zero, 1)

            lo, hi = slice(0, 64), slice(64, 128)
            pl.wait_ge(h0_ld, 16)
            pl.wait_ge(v_ev, 16)
            for c in range(NC5):
                here, nxt = HA[:, c], HA[:, c + 1]
                link(nc.gpsimd.tensor_tensor(rec[:, 0], Aj[:, 0, 0], here, ALU.mult))
                link(nc.gpsimd.tensor_tensor(rec[lo, 1], Aj[hi, 0, 1], here[hi], ALU.mult))
                link(nc.gpsimd.tensor_tensor(rec[hi, 1], Aj[lo, 0, 1], here[lo], ALU.mult))
                link(nc.gpsimd.tensor_tensor(nxt, nxt, rec[:, 0], ALU.add))
                link(nc.gpsimd.tensor_tensor(nxt, nxt, rec[:, 1], ALU.add))
            h0v = HA[:, COL_S0:COL_S0 + NS]
            link(nc.gpsimd.tensor_tensor(smp, bc(Aj[:, 1, 0], 1, NS), h0v, ALU.mult))
            link(nc.gpsimd.tensor_tensor(sst[:], sst[:], smp, ALU.add))
            link(nc.gpsimd.tensor_tensor(smp[lo], bc(Aj[hi, 1, 1], 1, NS), h0v[hi], ALU.mult))
            link(nc.gpsimd.tensor_tensor(smp[hi], bc(Aj[lo, 1, 1], 1, NS), h0v[lo], ALU.mult))
            nc.gpsimd.tensor_tensor(sst[:], sst[:], smp, ALU.add).then_inc(h_done, 1)
            pl.wait_ge(h_done, 1)
            pl.dma_start(a["o_s5p"].rearrange("r s g -> (r s) g"), HA[:, NC5]).then_inc(s5_out, 16)
            pl.dma_start(a["o_s5s"].rearrange("r s g -> (r s) g"), sst[:].rearrange("p b g -> p (b g)")).then_inc(s5_out, 16)

            pl.wait_ge(ea_out, 1)
            pl.wait_ge(y5_mm, 16)
            hin = a["ssm_in"].rearrange("b (i q) n -> b q i n", q=P)
            hout = a["o_ssm_s"].rearrange("b (i q) n -> b q i n", q=P)
            for b in range(2):
                pl.dma_start(h0b[b], hin[b]).then_inc(h0s_ld[b], 16)
            for b in range(NS):
                s = b % 2
                pl.wait_ge(bcs_ev, b + 2)
                link(nc.gpsimd.tensor_tensor(smu.rearrange("p (g i) n -> p g i n", g=2), bc(bcb[b][:, 0:2], 2, 4),
                                             bc(xds[:, :, b].rearrange("p (g i) -> p g i", g=2), 3, NSTATE), ALU.mult))
                pl.wait_ge(h0s_ld[s], 16 * (b // 2 + 1))
                link(nc.gpsimd.tensor_tensor(smt, h0b[s], bc(eA[:, :, b], 2, NSTATE), ALU.mult))
                nc.gpsimd.tensor_tensor(h0b[s], smt, smu, ALU.add).then_inc(hn_done, 1)
                pl.wait_ge(hn_done, b + 1)
                pl.dma_start(hout[b], h0b[s]).then_inc(h0s_st[s], 16)
                if 1 <= b < NS - 1:
                    pl.wait_ge(h0s_st[1 - s], 16 * ((b - 1) // 2 + 1))
                    pl.wait_ge(smv_done, b)
                    pl.dma_start(h0b[1 - s], hin[b + 1]).then_inc(h0s_ld[1 - s], 16)

            for q in range(4):
                pl.wait_ge(wo_hid, q + 1)
                nc.gpsimd.tensor_tensor(wo_lo[q % 2][:], wo[q % 2], wo_hi[q % 2][:].bitcast(F32), ALU.subtract).then_inc(wo_lod, 1)

            pl.wait_ge(tab_ev, 1)
            pl.wait_ge(x2_st, 80)
            for u in range(RING):
                link(nc.gpsimd.tensor_copy(idc[u], idx[:, u:u + 1]))
                nc.gpsimd.indirect_dma_start(xg[u], None, x2_scr,
                                             bass.IndirectOffsetOnAxis(ap=idc[u], axis=0)).then_inc(gath[u], 16)
            nt = tile_bound(pl, slice(E, E + 1), E)
            with pl.Fori(0, (nt + RING - 1) // RING) as it:
                for u in range(RING):
                    pl.wait_ge(staged, it * RING + u + 1)
                    pl.nop(nofuse=True)
                    nc.gpsimd.tensor_copy(idc[u], idx[:, bass.ds(it * RING + u + RING, 1)]).then_inc(idc_done, 1)
                    pl.wait_ge(idc_done, it * RING + u + 1)
                    pl.nop(nofuse=True)
                    nc.gpsimd.indirect_dma_start(xg[u], None, x2_scr,
                                                 bass.IndirectOffsetOnAxis(ap=idc[u], axis=0)).then_inc(gath[u], 16)
            for u in range(RING):
                pl.wait_ge(gath[u], ((nt + RING - 1) // RING) * 16 + 16)
            for u in range(RING):
                pl.wait_ge(yst[u], ((nt + RING - 1) // RING) * 32 + 32)
            pl.nop(nofuse=True)
            for i, (t0, n) in enumerate(TT):
                for k in range(2):
                    nc.gpsimd.indirect_dma_start(G[2 * i + k][0:n], None, ye_scr[0:MAXT * T, :],
                                                 bass.IndirectOffsetOnAxis(ap=slot[0:n, i, k:k + 1], axis=0))\
                        .then_inc(gy[i], 16)

        @block.tensor
        def _(pe):
            mm = nc.tensor.matmul

            def wide(w):
                src = xn if w < 28 else yg
                pe.wait_ge(ring_full[w % 3], 16 * (w // 3 + 1))
                if w >= 2:
                    pe.wait_ge(wide_free[w % 2], w // 2)
                if w == 28:
                    pe.wait_ge(gelu_done, 8)
                b0 = 2 * (w % 2)
                for k in range(KD):
                    if w == 0:
                        pe.wait_ge(xn_done, k + 1)
                    for h, (t0, t1) in enumerate(HALVES):
                        last = mm(ps[:, b0 + h, 0:t1 - t0], ring[w % 3][:, k, :], src[:, k, t0:t1],
                                  start=k == 0, stop=k == KD - 1)
                last.then_inc(wide_done, 1)

            def mean_square(src, done, each, tiles=KD):
                for k in range(tiles):
                    if each is not None:
                        pe.wait_ge(each, k + 1)
                    for h, (t0, t1) in enumerate(HALVES):
                        last = mm(ps[:, 4 + h, 0:t1 - t0], ones[:], src[:, k, t0:t1], start=k == 0, stop=k == tiles - 1)
                last.then_inc(done, 1)

            pe.wait_ge(ones_set, 1)
            mean_square(sq0, ms_done, sq_done)
            for w in range(6):
                wide(w)
            pe.wait_ge(q_done, 1)
            Qf = Qs.rearrange("p j g -> p (j g)")
            for i in range(4):
                last = nc.tensor.transpose(ps[:, 6, i * P:(i + 1) * P], Qf[:, i * P:(i + 1) * P], ident)
            last.then_inc(qt_mm, 1)
            for w in range(6, 8):
                wide(w)
            pe.wait_ge(wp_done, 1)
            pe.wait_ge(qt_ev, 1)
            for gq in range(16):
                for r in range(4):
                    g = 4 * gq + r
                    last = mm(ps[32 * r:32 * r + 32, 4 + gq // 4, (gq % 4) * P:(gq % 4) * P + P],
                              Bb[:, g * C5:(g + 2) * C5], Wp[:, g, 0:J, :], start=True, stop=True)
            last.then_inc(k_mm, 1)
            for w in range(8, 12):
                wide(w)
            pe.wait_ge(u_ld, 160)
            pe.wait_ge(k_ev, 1)

            def state_inputs(rd):
                if rd % 8 == 0:
                    pe.wait_ge(v_done, rd // 8 + 1)
                if rd >= 2:
                    pe.wait_ge(v_ev, rd - 1)
                for q in range(4):
                    g = 4 * rd + q
                    last = mm(ps[:, 4 + rd % 2, q * WIN:q * WIN + WIN], Vm[:, g % 32], U[:, g * UC:g * UC + WIN],
                              start=True, stop=True)
                last.then_inc(v_mm, 1)

            pe.wait_ge(ld_misc, 112)
            for h, (t0, t1) in enumerate(HALVES):
                for k in range(KD):
                    last = mm(ps[0:HEADS, 6 + h, 0:t1 - t0], wdt[:, k, :], xn[:, k, t0:t1],
                              start=k == 0, stop=k == KD - 1)
            last.then_inc(dt_mm, 1)
            for rd in range(8):
                state_inputs(rd)
            for w in (12, 13):
                wide(w)
            for rd in range(8, 16):
                state_inputs(rd)
            pe.wait_ge(dt_ev, 1)
            for i, (t0, n) in enumerate(TT):
                last = nc.tensor.transpose(ps[0:n, 6, i * HEADS:(i + 1) * HEADS], dt_raw[:, t0:t0 + n],
                                           cst[0:HEADS, C_ID:C_ID + HEADS])
            last.then_inc(dtt_mm, 1)
            for w in range(14, 20):
                wide(w)
            pe.wait_ge(t_ld, 16 * 32)
            pe.wait_ge(v_ev, 16)
            for rd in range(16):
                if rd >= 2:
                    pe.wait_ge(lc_ev, rd - 1)
                for q in range(4):
                    g = 4 * rd + q
                    last = mm(ps[:, 4 + rd % 2, q * WIN:q * WIN + WIN], Tm[:, g], U[:, g * UC:g * UC + WIN],
                              start=True, stop=True)
                last.then_inc(lc_mm, 1)
            pe.wait_ge(dt_done, 1)
            for h in range(HEADS):
                r, i = h % 2, h // 2
                last = mm(ps[64 * r:64 * r + 64, 6, 256 + i * NS:256 + (i + 1) * NS],
                          dtv[0:24, 4, h:h + 1].broadcast_to([24, HD]), cst[0:24, C_ID + 16:C_ID + 24],
                          start=True, stop=True)
            last.then_inc(ds_mm, 1)
            pe.wait_ge(ds_ev, 1)
            pe.wait_ge(lc_ev, 16)

            def state_outputs():
                pe.wait_ge(h_done, 1)
                pe.wait_ge(y_ev, 2)
                HAv = arena[:, HA_off:HA_off + WIN * G5].rearrange("p (c g) -> p g c", g=G5)
                for rd in range(16):
                    if rd >= 2:
                        pe.wait_ge(y5_ev, rd - 1)
                    for q in range(4):
                        g = 4 * rd + q
                        last = mm(ps[:, 4 + rd % 2, q * WIN:q * WIN + WIN], Wp[:, g, 1:J + 1, :], HAv[:, g, :],
                                  start=True, stop=True)
                    last.then_inc(y5_mm, 1)

            def sample_bc():
                pe.wait_ge(st_ev, 2)
                for i in range(4):
                    last = nc.tensor.transpose(ps[0:24, 7, i * P:(i + 1) * P], xcB[:, i, 4 * P:N], ident)
                last.then_inc(bcs_mm, 1)
                pe.wait_ge(y5_ev, 16)
                for b in range(NS):
                    pe.wait_ge(bcs_ev, max(1, b - 2))
                    mm(ps[:, 4 + b % 4, :], cst[0:24, C_ID + 16 + b:C_ID + 17 + b].broadcast_to([24, P]), bts[0:24],
                       start=True, stop=True).then_inc(bcs_mm, 1)
                pe.wait_ge(bcs_ev, 9)

            def ssd_a(c):
                t0, n = CH[c]
                if c >= 1:
                    pe.wait_ge(y_ev, c)
                    pe.wait_ge(st_ev, c)
                for i in range(8):
                    nc.tensor.transpose(ps[0:n, 4 + i // 4, (i % 4) * P:(i % 4 + 1) * P], xcX[:, i, t0:t0 + n], ident)
                for i in range(2):
                    nc.tensor.transpose(ps[0:n, 6, i * P:(i + 1) * P], xcB[:, i, t0:t0 + n], ident)
                mm(ps[0:n, 7, 0:16], tri[0:n, 0:n], dav[0:n, c, :], start=True, stop=True)
                mm(ps[:, 7, 16:32], ones[0:n, :], dav[0:n, c, :], start=True, stop=True)
                for g in range(2):
                    last = mm(ps[0:n, 7, 128 + g * P:128 + g * P + n], xcB[:, g, t0:t0 + n], xcB[:, 2 + g, t0:t0 + n],
                              start=True, stop=True)
                last.then_inc(sa_mm, 1)

            def ssd_b(c):
                n = CH[c][1]
                pe.wait_ge(sa_evd, c + 1)
                pe.wait_ge(sa_eva, c + 1)
                for h in range(HEADS):
                    last = mm(ps[:, 4 + h // 4, (h % 4) * P:(h % 4) * P + n],
                              dav[0:n, c, h:h + 1].broadcast_to([n, P]), tri[0:n, 0:n], start=True, stop=True)
                last.then_inc(cb_mm, 1)

            def ssd_c(c):
                n = CH[c][1]
                pe.wait_ge(m_done, c + 1)
                if c:
                    pe.wait_ge(cs_done, c)
                for i in range(8):
                    for r in range(2):
                        h = 2 * i + r
                        last = mm(ps[64 * r:64 * r + 64, 4 + i // 4, (i % 4) * P:(i % 4) * P + n],
                                  xdt[0:n, h, :], Lm[0:n, h, 0:n], start=True, stop=c == 0)
                    for r in range(2) if c else ():
                        h = 2 * i + r
                        last = mm(ps[64 * r:64 * r + 64, 4 + i // 4, (i % 4) * P:(i % 4) * P + n],
                                  Hs[:, h, :], E2[:, h, 0:n], start=False, stop=True)
                last.then_inc(y_mm, 1)
                for g in range(2):
                    last = mm(ps[:, 6 + g, :], btok[0:n, g, :], xde[0:n, 8 * g:8 * g + 8, :], start=True, stop=True)
                last.then_inc(st_mm, 1)

            pe.wait_ge(silu_done, XBC)
            for c in range(5):
                ssd_a(c)
                if c < 4:
                    wide(20 + 2 * c)
                ssd_b(c)
                if c < 4:
                    wide(21 + 2 * c)
                ssd_c(c)
                if c == 1:
                    state_outputs()
                    sample_bc()
            for w in range(28, 32):
                wide(w)
            pe.wait_ge(sqt_done, 1)
            mean_square(sq, ms_done, None, 1)
            for w in range(32, 36):
                wide(w)

            def project_tile(q, i):
                yh, yl, wh, wl = y_hi[q // 2], y_lo[q // 2], wo_hi[q % 2], wo_lo[q % 2]
                if i == 0:
                    pe.wait_ge(wo_lod, q + 1)
                t0, n = TT[i]
                o = 5 * q + i
                if o >= 4:
                    pe.wait_ge(o_ev, o - 3)
                for k in range(KD):
                    for j, (y_, w_) in enumerate(((yh, wh), (yh, wl), (yl, wh))):
                        last = mm(ps[0:n, o % 4, :], y_[:, k, t0:t0 + n], w_[:, k, :],
                                  start=k == 0 and j == 0, stop=k == KD - 1 and j == 2)
                last.then_inc(o_mm, 1)

            def project(q):
                for i in range(5):
                    project_tile(q, i)

            pe.wait_ge(wide_free[0], 18)
            pe.wait_ge(wide_free[1], 18)
            pe.wait_ge(ys_done, 1)
            project(0)
            pe.wait_ge(sqt_done, 2)
            mean_square(sq, ms_done, None, 1)
            project(1)
            pe.wait_ge(ys_done, 2)
            project(2)

            def x2_transposes(i):
                n = TT[i][1]
                pe.wait_ge(x2_done, i + 1)
                if i:
                    pe.wait_ge(x2t_ev, i)
                for k in range(KD):
                    last = nc.tensor.transpose(ps[:, 4 + k // 4, (k % 4) * P:(k % 4) * P + n], x2[0:n, k * P:(k + 1) * P],
                                               cst[0:n, C_ID:C_ID + n])
                last.then_inc(x2t_mm, 1)

            def logits(i):
                n = TT[i][1]
                if i == 0:
                    pe.wait_ge(moe_ld, 32)
                else:
                    pe.wait_ge(lg_ev, i)
                pe.wait_ge(x2t_ev, i + 1)
                for k in range(KD):
                    last = mm(ps[0:36, 6, 0:n], wr[:, k, :], x2T[:, k, 0:n], start=k == 0, stop=k == KD - 1)
                last.then_inc(lg_mm, 1)

            def logits_back(i):
                n = TT[i][1]
                pe.wait_ge(lg_ev, i + 1)
                nc.tensor.transpose(ps[0:n, 7, i * 36:(i + 1) * 36], lgs[:, 0:n], cst[0:36, C_ID:C_ID + 36]).then_inc(lgt_mm, 1)

            for i in range(8):
                if i < 5:
                    project_tile(3, i)
                if 0 <= i - 3:
                    logits_back(i - 3)
                if 0 <= i - 2 < 5:
                    logits(i - 2)
                if 0 <= i - 1 < 5:
                    x2_transposes(i - 1)
            pe.wait_ge(ob_done, 1)
            for i in range(6):
                for j in range(min(i, 4) + 1):
                    last = mm(ps[:, 7, 256 + i * E:256 + (i + 1) * E], onb[:, 1 if j == i else 0, :], Ob[:, j, :],
                              start=j == 0, stop=j == min(i, 4))
            last.then_inc(rank_mm, 1)
            pe.wait_ge(oh_done, 1)
            for j in range(10):
                last = mm(ps[0:T, 6, 0:IDXC], oh_row[:, j, :], oh_tile[:, j, :], start=j == 0, stop=j == 9)
            last.then_inc(tab_mm, 1)

            def x_transposes(q):
                pe.wait_ge(staged, q + 1)
                pe.nop(nofuse=True)
                for k in range(KD):
                    last = nc.tensor.transpose(ps[:, 2, k * T:(k + 1) * T], xst[:, k::KD], cst[0:T, C_ID:C_ID + T])
                last.then_inc(xtr, 1)

            pe.wait_ge(slot_done, 1)
            for s_ in (xtr, htr, dmm):
                pe.sem_inc(s_, 1)
            x_transposes(0)

            def expert(s, turn, lo, hi):
                q0 = tile_bound(pe, lo, 0)
                q1 = tile_bound(pe, hi, 1)
                with pe.Fori(q0, q1) as q:
                    pe.wait_ge(xev, q + 1)
                    pe.wait_ge(wg_ld[s], turn * 16 + 16)
                    pe.wait_ge(silu, q + 1)
                    for k in range(KD):
                        for r in range(2):
                            last = mm(ps[64 * r:64 * r + 64, 0, 0:256], xt[:, k, :],
                                      Wg[s][:, k, 256 * r:256 * r + 256], start=k == 0, stop=k == KD - 1)
                    last.then_inc(gmm, 1)
                    pe.wait_ge(wu_ld[s], turn * 16 + 16)
                    pe.wait_ge(hr, q + 1)
                    for k in range(KD):
                        for r in range(2):
                            last = mm(ps[64 * r:64 * r + 64, 1, 0:256], xt[:, k, :],
                                      Wu[s][:, k, 256 * r:256 * r + 256], start=k == 0, stop=k == KD - 1)
                    last.then_inc(umm, 1)
                    x_transposes(q + 1)
                    pe.wait_ge(hr, q + 2)
                    pe.nop(nofuse=True)
                    for j in range(2):
                        last = nc.tensor.transpose(ps[:, 3, j * P:(j + 1) * P], hh[:, j * P:(j + 1) * P], ident)
                    last.then_inc(htr, 1)
                    pe.wait_ge(hev, q + 1)
                    pe.wait_ge(wd_ld[s], turn * 16 + 16)
                    pe.wait_ge(yev, q + 1)
                    for k in range(4):
                        for r in range(2):
                            last = mm(ps[64 * r:64 * r + 64, 4, :], ht[:, k % 2, 64 * (k // 2):64 * (k // 2) + 64],
                                      Wd[s][:, k, 512 * r:512 * r + 512], start=k == 0, stop=k == 3)
                    last.then_inc(dmm, 1)

            with pe.Fori(0, E_LOOP) as ep:
                for s in range(WBUF):
                    e = ep * WBUF + s
                    expert(s, ep, bass.ds(e, 1), bass.ds(e + 1, 1))
            for e in range(E_LOOP * WBUF, E):
                expert(e % WBUF, e // WBUF, slice(e, e + 1), slice(e + 1, e + 2))
            pe.sem_inc(xtr, RING - 1)
            pe.wait_ge(yev, tile_bound(pe, slice(E, E + 1), E) + 1)
            pe.sem_inc(gmm, RING - 1)
            pe.sem_inc(dmm, RING - 1)

        @block.scalar
        def _(ac):
            act_ = nc.scalar.activation
            cnt = [0]

            def link(ins):
                cnt[0] += 1
                ins.then_inc(act, 1)
                ac.wait_ge(act, cnt[0])

            for k in range(KD):
                if k % 4 == 0:
                    ac.wait_ge(ld_x[k // 4], 16)
                act_(sq0[:, k, :], xT[:, k, :], ACT.Square).then_inc(sq_done, 1)
            ac.wait_ge(root_in, 1)
            act_(rms0, rms0, ACT.Sqrt).then_inc(root_out, 1)
            ac.wait_ge(ld_s5, 16)
            act_(tv(3), tv(2), ACT.Exp).then_inc(s5_act, 1)
            ac.wait_ge(s5_dve, 1)
            act_(tv(5), tv(4), ACT.Exp).then_inc(s5_act, 1)
            ac.wait_ge(s5_dve, 2)
            act_(tv(8), tv(6), ACT.Sin).then_inc(s5_act, 1)
            act_(tv(9), tv(7), ACT.Sin).then_inc(s5_act, 1)

            def evac_u(w):
                ac.wait_ge(wide_done, w + 1)
                if w >= 2:
                    ac.wait_ge(u_st[w % 2], 16 * (w // 2))
                b0 = 2 * (w % 2)
                dst = uD[w % 2]
                dj = dst[:, 0:NP_].rearrange("p (j m) -> p j m", j=J)
                act_(dj[:, :, 0:33], ps[:, b0, 0:SPLIT].rearrange("p (m j) -> p j m", j=J), ACT.Copy)
                act_(dj[:, :, 33:66], ps[:, b0 + 1, 0:SPLIT].rearrange("p (m j) -> p j m", j=J), ACT.Copy)
                act_(dst[:, NP_:N], ps[:, b0 + 1, SPLIT:N - SPLIT], ACT.Copy).then_inc(wide_free[w % 2], 1)
                ac.wait_ge(wide_free[w % 2], w // 2 + 1)
                ac.dma_start(u_scr[w * P:(w + 1) * P, :], dst).then_inc(u_st[w % 2], 16)

            for w in range(8):
                evac_u(w)
            ac.wait_ge(k_mm, 1)
            for i in range(4):
                last = act_(Kx[:, 4 * i:4 * i + 4], ps[:, 4 + i, :].rearrange("p (q j c) -> p q j c", q=4, j=J), ACT.Copy)
            last.then_inc(k_ev, 1)

            def raw_evac(w):
                i = w - 8
                ac.wait_ge(wide_done, w + 1)
                if i >= 2:
                    ac.wait_ge(conv_done, i - 1)
                b0 = 2 * (w % 2)
                dst = raw[i % 2]
                act_(dst[:, 3:3 + SPLIT], ps[:, b0, 0:SPLIT], ACT.Copy)
                act_(dst[:, 3 + SPLIT:3 + NP_], ps[:, b0 + 1, 0:SPLIT], ACT.Copy)
                sm = dst[:, 531:563].rearrange("p (b j) -> p b j", j=CONV)
                act_(sm[:, :, 3], ps[:, b0 + 1, SPLIT:N - SPLIT], ACT.Copy).then_inc(wide_free[w % 2], 1)
                f = conv_tile(i)
                act_(sm[:, :, 0:3].rearrange("p b j -> p j b"), scv[:, :, f, :], ACT.Copy).then_inc(raw_done, 1)

            def conv_silu(i):
                ac.wait_ge(conv_done, i + 1)
                dst = conv_dst(i)
                act_(dst, dst, ACT.Silu).then_inc(silu_done, 1)

            ac.wait_ge(ld_misc, 112)
            for i in range(4):
                raw_evac(8 + i)
                if 0 < i < 3:
                    conv_silu(i - 1)

            def states_evac(rd):
                ac.wait_ge(v_mm, rd + 1)
                src = ps[:, 4 + rd % 2, 0:4 * WIN].rearrange("p (q c) -> p q c", q=4)
                act_(part(HA_off, 76, G5)[:, 1:67, 4 * rd:4 * rd + 4].rearrange("p c g -> p g c"), src[:, :, 0:NC5], ACT.Copy)
                act_(sst[:, :, 4 * rd:4 * rd + 4].rearrange("p c g -> p g c"), src[:, :, COL_S7:COL_S7 + NS],
                     ACT.Copy).then_inc(v_ev, 1)

            for rd in range(8):
                states_evac(rd)
            conv_silu(2)
            conv_silu(3)
            for i in (4, 5):
                raw_evac(8 + i)
            for rd in range(8, 16):
                states_evac(rd)
            ac.wait_ge(s5_dve, 3)
            act_(sp_u, sp_u, ACT.Exp)
            act_(arow[:], arow[:], ACT.Exp)
            act_(aexp[:], pf[:, PF_ALOG:PF_ALOG + 8], ACT.Exp).then_inc(s5_act, 1)
            conv_silu(4)
            for i in range(6, XBC):
                raw_evac(8 + i)
                conv_silu(i - 1)
            conv_silu(XBC - 1)
            Ug = U[:, 0:G5 * UC].rearrange("p (g c) -> p g c", g=G5)
            for rd in range(16):
                ac.wait_ge(lc_mm, rd + 1)
                act_(Ug[:, 4 * rd:4 * rd + 4, 0:YC],
                     ps[:, 4 + rd % 2, 0:4 * WIN].rearrange("p (q c) -> p q c", q=4)[:, :, 0:YC], ACT.Copy).then_inc(lc_ev, 1)
            ac.wait_ge(ds_ev, 1)
            act_(eA[:], eA[:], ACT.Exp).then_inc(ea_out, 1)

            def z_evac(w):
                ac.wait_ge(wide_done, w + 1)
                b0 = 2 * (w % 2)
                act_(zT[:, w - 20, 0:SPLIT], ps[:, b0, 0:SPLIT], ACT.Copy)
                act_(zT[:, w - 20, SPLIT:N], ps[:, b0 + 1, 0:N - SPLIT], ACT.Copy).then_inc(wide_free[w % 2], 1)

            for c in range(5):
                n = CH[c][1]
                ac.wait_ge(sa_mm, c + 1)
                act_(btok[0:n], ps[0:n, 6, 0:2 * P].rearrange("p (a q) -> p a q", a=2), ACT.Copy).then_inc(sa_eva, 1)
                ac.wait_ge(de_in, c + 1)
                act_(dev[:], dev[:], ACT.Exp).then_inc(de_out, 1)
                if c < 4:
                    z_evac(20 + 2 * c)
                ac.wait_ge(cb_mm, c + 1)
                for i in range(4):
                    ac.wait_ge(l_in, 4 * c + i + 1)
                    last = act_(E2[:, 4 * i:4 * i + 4, 0:n],
                                ps[:, 4 + i, :].rearrange("p (h l) -> p h l", h=4)[:, :, 0:n], ACT.Exp)
                last.then_inc(e2_done, 1)
                act_(Lm[0:n, :, 0:n], Lm[0:n, :, 0:n], ACT.Exp).then_inc(l_exp, 1)
                if c < 4:
                    z_evac(21 + 2 * c)
                if c == 1:
                    ac.wait_ge(bcs_mm, 1)
                    ac.wait_ge(s5_out, 32)
                    act_(bts[0:24], ps[0:24, 7, :].rearrange("p (a q) -> p a q", a=4), ACT.Copy).then_inc(bcs_ev, 1)
                    for b in range(NS):
                        ac.wait_ge(bcs_mm, b + 2)
                        act_(bcb[b], ps[:, 4 + b % 4, :].rearrange("p (a q) -> p a q", a=4), ACT.Copy).then_inc(bcs_ev, 1)
                if c == 3:
                    ac.wait_ge(yraw_ld, 16)
                    for i in range(8):
                        act_(yg[:, i, 0:NP_].rearrange("p (m j) -> p m j", j=J),
                             yraw[:, i, 0:NP_].rearrange("p (j m) -> p m j", j=J), ACT.Gelu_apprx_tanh)
                        act_(yg[:, i, NP_:N], yraw[:, i, NP_:N], ACT.Gelu_apprx_tanh).then_inc(gelu_done, 1)
            act_(zT, zT, ACT.Silu).then_inc(zs_done, 1)

            ac.wait_ge(gt_done, 1)
            for k in range(KD):
                act_(sq[:, k, :], ySSD[:, k, :], ACT.Square).then_inc(sq_done, 1)

            def norm_root(i):
                ac.wait_ge(root_in, i + 2)
                act_(rmsN, rmsN, ACT.Sqrt).then_inc(root_out, 1)

            def high_parts(i, src):
                for k in range(KD):
                    ac.wait_ge(yn_done, 8 * i + k + 1)
                    act_(y_hi[i][:, k, :], src[:, k, :], ACT.Copy).then_inc(yh_done, 1)

            def wo_high(q):
                ac.wait_ge(wo_ld[q % 2], 16 * (q // 2 + 1))
                act_(wo_hi[q % 2][:], wo[q % 2], ACT.Copy).then_inc(wo_hid, 1)

            for s_ in range(2):
                ac.wait_ge(h0s_st[s_], 64)
            for w in range(28, 36):
                ac.wait_ge(wide_done, w + 1)
                b0 = 2 * (w % 2)
                i = w - 28
                act_(sig[:, i, 0:SPLIT], ps[:, b0, 0:SPLIT], ACT.Sigmoid, bias=pf[:, PF_BGLU + i:PF_BGLU + i + 1])
                act_(sig[:, i, SPLIT:N], ps[:, b0 + 1, 0:N - SPLIT], ACT.Sigmoid,
                     bias=pf[:, PF_BGLU + i:PF_BGLU + i + 1]).then_inc(wide_free[w % 2], 1)
                if w == 29:
                    wo_high(0)
                if w == 31:
                    norm_root(0)
                if w == 32:
                    high_parts(0, ySSD)
            ac.wait_ge(ms_done, 2)
            for k in range(KD):
                ac.wait_ge(y2_done, k + 1)
                act_(sq[:, k, :], sig[:, k, :], ACT.Square).then_inc(sq_done, 1)
            wo_high(1)
            norm_root(1)
            high_parts(1, sig)
            wo_high(2)
            wo_high(3)

            def moe_norm(i):
                n = TT[i][1]
                ac.wait_ge(o_ev, 15 + i + 1)
                if i:
                    ac.wait_ge(xs_sq, i)
                act_(junk[0:n], x1[i][0:n], ACT.Square, accum_out=ssum[0:n, i:i + 1]).then_inc(xs_sq, 1)
                ac.wait_ge(root_in, 4 + i)
                act_(ssum[:, i:i + 1], ssum[:, i:i + 1], ACT.Sqrt).then_inc(root_out, 1)

            def x2_store(i):
                t0, n = TT[i]
                ac.wait_ge(x2_done, i + 1)
                ac.dma_start(x2_scr[t0:t0 + n, :], x2[0:n, :]).then_inc(x2_st, 16)

            def x2_evac(i):
                n = TT[i][1]
                ac.wait_ge(x2t_mm, i + 1)
                if i:
                    ac.wait_ge(lg_mm, i)
                for h in range(2):
                    last = act_(x2T[:, 4 * h:4 * h + 4, 0:n],
                                ps[:, 4 + h, :].rearrange("p (k t) -> p k t", k=4)[:, :, 0:n], ACT.Copy)
                last.then_inc(x2t_ev, 1)

            def logits_evac(i):
                n = TT[i][1]
                ac.wait_ge(lg_mm, i + 1)
                if i:
                    ac.wait_ge(lgt_mm, i)
                act_(lgs[:, 0:n], ps[0:36, 6, 0:n], ACT.Identity, bias=brc[:]).then_inc(lg_ev, 1)

            for i in range(7):
                if i < 5:
                    moe_norm(i)
                if 0 <= i - 2:
                    logits_evac(i - 2)
                if i < 5:
                    x2_store(i)
                if 0 <= i - 1 < 5:
                    x2_evac(i - 1)
            ac.wait_ge(r_in, 1)
            act_(rexp, rexp, ACT.Exp).then_inc(r_out, 1)
            ac.wait_ge(r_in, 2)
            act_(rdif, rdif, ACT.Exp).then_inc(r_out, 1)

            ac.wait_ge(slot_done, 1)
            ac.wait_ge(ye_zero, 32)
            nt = tile_bound(ac, slice(E, E + 1), E)
            for s_, v_ in ((silu, 1), (yev, 1), *((y, 32) for y in yst)):
                ac.sem_inc(s_, v_)
            ac.wait_ge(gath[0], 16)
            act_(xst, xg[0], ACT.Copy).then_inc(staged, 1)
            with ac.Fori(0, (nt + RING - 1) // RING) as it:
                for u in range(RING):
                    q = it * RING + u
                    ac.wait_ge(gmm, q + 1)
                    ac.wait_ge(hr, q + 1)
                    act_(sg, ps[:, 0, 0:256], ACT.Silu).then_inc(silu, 1)
                    ac.wait_ge(xtr, q + 2)
                    ac.wait_ge(gath[(u + 1) % RING], it * 16 + 16 + 16 * ((u + 1) // RING))
                    act_(xst, xg[(u + 1) % RING], ACT.Copy).then_inc(staged, 1)
                    ac.wait_ge(dmm, q + 2)
                    ac.wait_ge(yst[u], it * 32 + 32)
                    act_(yo[u], ps[:, 4, :], ACT.Copy).then_inc(yev, 1)
                    ac.wait_ge(yev, q + 2)
                    for r in range(2):
                        ac.dma_start(ye_scr[bass.ds(q * T, T), r * 512:r * 512 + 512],
                                     yo[u][64 * r:64 * r + 64, :]).then_inc(yst[u], 16)
                ac.nop(nofuse=True)
            ac.nop(nofuse=True)
            for i, (t0, n) in enumerate(TT):
                ac.wait_ge(fin_done, i + 1)
                act_(G[2 * i][0:n], x1[i][0:n], ACT.Square, accum_out=ssum[0:n, i:i + 1]).then_inc(xs_sq, 1)
                ac.wait_ge(root_in, 9 + i)
                act_(ssum[:, i:i + 1], ssum[:, i:i + 1], ACT.Sqrt).then_inc(root_out, 1)

        @block.vector
        def _(dv):
            V = nc.vector
            cnt = [0]

            def link(ins):
                cnt[0] += 1
                ins.then_inc(dve, 1)
                dv.wait_ge(dve, cnt[0])

            def tt(o, x, y, op):
                link(V.tensor_tensor(o, x, y, op))

            def ts(o, x, s1, s2, op0, op1=None):
                if op1 is None:
                    link(V.tensor_scalar(o, x, s1, None, op0))
                else:
                    link(V.tensor_scalar(o, x, s1, s2, op0, op1))

            def stt(o, x, s, y, op0, op1):
                link(V.scalar_tensor_tensor(o, x, s, y, op0, op1))

            V.memset(ones[:], 1.0).then_inc(ones_set, 1)
            V.memset(raw[0][:, 0:3], 0.0)
            V.memset(raw[1][:, 0:3], 0.0)
            link(V.memset(dtv[:], 0.0))
            link(V.memset(ssum[:], 0.0))
            dv.wait_ge(ld_const, 32)

            def root(rms, want):
                for h, (t0, t1) in enumerate(HALVES):
                    last = V.tensor_scalar(rms[:, t0:t1], ps[:, 4 + h, 0:t1 - t0], 1.0 / D, EPS, ALU.mult, ALU.add)
                last.then_inc(root_in, 1)
                dv.wait_ge(root_out, want)
                link(V.reciprocal(rms, rms))

            dv.wait_ge(ms_done, 1)
            root(rms0, 1)
            link(V.memset(dev[:], 0.0))
            for k in range(KD):
                V.scalar_tensor_tensor(xn[:, k, :], xT[:, k, :], pf[:, PF_GMIX + k:PF_GMIX + k + 1], rms0,
                                       ALU.mult, ALU.mult).then_inc(xn_done, 1)
            dv.wait_ge(s5_act, 1)
            tt(tv(4), tv(0), tv(3), ALU.mult)
            V.tensor_tensor(tv(10), tv(1), tv(3), ALU.mult).then_inc(s5_dve, 1)
            dv.wait_ge(s5_dve, 1)
            ts(tv(11), tv(10), 1.0 / (2 * np.pi), MAGIC, ALU.mult, ALU.add)
            ts(tv(11), tv(11), MAGIC, None, ALU.subtract)
            for part_of in (TWO_PI_HI, TWO_PI_MID, TWO_PI_LO):
                stt(tv(10), tv(11), -float(part_of), tv(10), ALU.mult, ALU.add)
            ts(tv(6), tv(10), PI_F, -PI_F, ALU.min, ALU.max)
            ts(tv(7), tv(6), -1.0, None, ALU.mult)
            tt(tv(7), tv(7), tv(6), ALU.max)
            V.tensor_scalar(tv(7), tv(7), -1.0, float(np.pi / 2), ALU.mult, ALU.add).then_inc(s5_dve, 1)
            dv.wait_ge(s5_act, 4)
            tt(Pre[:, 1, :], tv(5), tv(9), ALU.mult)
            tt(Pim[:, 1, :], tv(5), tv(8), ALU.mult)
            link(V.memset(Pre[:, 0, :], 1.0))
            link(V.memset(Pim[:, 0, :], 0.0))
            ts(tv(4), Pre[:, 1, :], 1.0, None, ALU.subtract)
            tt(tv(5), tv(0), tv(0), ALU.mult)
            tt(tv(6), tv(1), tv(1), ALU.mult)
            tt(tv(5), tv(5), tv(6), ALU.add)
            link(V.reciprocal(tv(5), tv(5)))
            tt(tv(6), tv(4), tv(0), ALU.mult)
            tt(tv(7), Pim[:, 1, :], tv(1), ALU.mult)
            tt(tv(6), tv(6), tv(7), ALU.add)
            tt(tv(8), tv(6), tv(5), ALU.mult)
            tt(tv(6), Pim[:, 1, :], tv(0), ALU.mult)
            tt(tv(7), tv(4), tv(1), ALU.mult)
            tt(tv(6), tv(6), tv(7), ALU.subtract)
            tt(tv(9), tv(6), tv(5), ALU.mult)
            for m in (1, 2, 4):
                lo, hi = slice(1, m + 1), slice(m + 1, 2 * m + 1)
                br, bi = bc(Pre[:, m, :], 1, m), bc(Pim[:, m, :], 1, m)
                w0 = pw_t[:, 0:m * G5].rearrange("p (t g) -> p t g", g=G5)
                tt(Pre[:, hi], Pre[:, lo], br, ALU.mult)
                tt(w0, Pim[:, lo], bi, ALU.mult)
                tt(Pre[:, hi], Pre[:, hi], w0, ALU.subtract)
                tt(Pim[:, hi], Pre[:, lo], bi, ALU.mult)
                tt(w0, Pim[:, lo], br, ALU.mult)
                tt(Pim[:, hi], Pim[:, hi], w0, ALU.add)
            V.memset(csv[:], 0.0).then_inc(pow_done, 1)
            sgn, m0, m1 = (cst[:, x:x + 1] for x in (C_SGN, C_M0, C_M1))
            for o, m in enumerate((J, 1)):
                link(V.tensor_copy(Aj[:, o, 0, :], Pre[:, m, :]))
                ts(Aj[:, o, 1, :], Pim[:, m, :], sgn, None, ALU.mult)
            ts(tv(4), tv(8), m0, None, ALU.mult)
            stt(tv(4), tv(9), m1, tv(4), ALU.mult, ALU.add)
            ts(tv(5), tv(8), m1, None, ALU.mult)
            ts(tv(6), tv(9), m0, None, ALU.mult)
            tt(tv(5), tv(5), tv(6), ALU.subtract)
            for j in range(J):
                tt(Qs[:, j, :], Pre[:, J - 1 - j, :], tv(4), ALU.mult)
                tt(tv(7), Pim[:, J - 1 - j, :], tv(5), ALU.mult)
                tt(Qs[:, j, :], Qs[:, j, :], tv(7), ALU.add)
            V.memset(csv[:], 0.0).then_inc(q_done, 1)
            dv.wait_ge(ld_stk, 16)
            ts(tv(6), tv(9), sgn, -1.0, ALU.mult, ALU.mult)
            tt(stk[:, 2], stk[:, 2], bc(tv(8), 2, C5), ALU.mult)
            tt(stk[:, 3], stk[:, 3], bc(tv(6), 2, C5), ALU.mult)
            tt(stk[:, 2], stk[:, 2], stk[:, 3], ALU.add)
            ts(stk[:, 0], stk[:, 0], sgn, None, ALU.mult)
            tt(Wp, bc(stk[:, 0], 2, J + 1), bc(Pre.rearrange("p t g -> p g t"), 3, C5), ALU.mult)
            dv.wait_ge(wt_done, 1)
            V.tensor_tensor(Wp, Wp, Wt, ALU.subtract).then_inc(wp_done, 1)
            dv.wait_ge(ld_misc, 112)
            for r in range(4):
                q_ = slice(32 * r, 32 * r + 32)
                tt(dkt[q_], bc(cst[q_, C_ID + 32 * r:C_ID + 32 * r + C5], 1, 16), bc(dK[q_, :], 2, C5), ALU.mult)
            dv.wait_ge(qt_mm, 1)
            V.tensor_copy(qt, ps[:, 6, :].rearrange("p (b r) -> p b r", b=4)).then_inc(qt_ev, 1)
            dv.wait_ge(k_ev, 1)
            V.tensor_tensor(Kx[:, :, 0, :], Kx[:, :, 0, :], dkt, ALU.add).then_inc(k_ev, 1)

            def make_v(half):
                dv.wait_ge(qb_ld[half], 256)
                if half:
                    dv.wait_ge(v_mm, 8)
                tt(Vm, QB, BT, ALU.mult)
                tt(Vm[:, :, 0, :], Vm[:, :, 0, :], Vm[:, :, 1, :], ALU.subtract)
                tt(QB, QB, BT[:, :, ::-1, :], ALU.mult)
                V.tensor_tensor(Vm[:, :, 1, :], QB[:, :, 0, :], QB[:, :, 1, :], ALU.add).then_inc(v_done, 1)

            def conv(i):
                f = conv_tile(i)
                src, dst = raw[i % 2], conv_dst(i)
                w_ = [pf[:, PF_CW + 4 * f + k:PF_CW + 4 * f + k + 1] for k in range(CONV)]
                b_ = pf[:, PF_CB + f:PF_CB + f + 1]
                sm = src[:, 531:563].rearrange("p (b j) -> p b j", j=CONV)
                dv.wait_ge(raw_done, i + 1)
                ts(dst[:, 0:NP_], src[:, 0:NP_], w_[0], b_, ALU.mult, ALU.add)
                ts(dst[:, NP_:N], sm[:, :, 0], w_[0], b_, ALU.mult, ALU.add)
                for k in range(1, CONV):
                    stt(dst[:, 0:NP_], src[:, k:k + NP_], w_[k], dst[:, 0:NP_], ALU.mult, ALU.add)
                    stt(dst[:, NP_:N], sm[:, :, k], w_[k], dst[:, NP_:N], ALU.mult, ALU.add)
                link(V.tensor_copy(ncp[:, f, :], src[:, NP_:NP_ + 3]))
                V.tensor_copy(ncs[:, f], sm[:, :, 3]).then_inc(conv_done, 1)

            conv(0)
            conv(1)
            make_v(0)
            conv(2)
            conv(3)
            make_v(1)
            dv.wait_ge(dt_mm, 1)
            for h, (t0, t1) in enumerate(HALVES):
                link(V.tensor_scalar(dt_raw[:, t0:t1], ps[0:HEADS, 6 + h, 0:t1 - t0], dtb[:], None, ALU.add))
            V.memset(csv[:], 0.0).then_inc(dt_ev, 1)
            dv.wait_ge(dtt_mm, 1)
            link(V.tensor_copy(dtv[:, 0:4, :], ps[:, 6, 0:64].rearrange("p (i h) -> p i h", i=4)))
            link(V.tensor_copy(dtv[0:24, 4, :], ps[0:24, 6, 64:80]))
            dvf, sps, spz = dtv[:].rearrange("p i h -> p (i h)"), sp_s, sp_z
            ts(sp_u, dvf, -1.0, None, ALU.mult)
            V.tensor_tensor(sp_u, sp_u, dvf, ALU.min).then_inc(s5_dve, 1)
            dv.wait_ge(s5_act, 5)
            ts(sps, sp_u, 2.0, None, ALU.add)
            link(V.reciprocal(sps, sps))
            tt(sps, sps, sp_u, ALU.mult)
            tt(spz, sps, sps, ALU.mult)
            link(V.memset(sp_u, 1.0 / 17))
            for m in (15, 13, 11, 9, 7, 5, 3):
                tt(sp_u, sp_u, spz, ALU.mult)
                ts(sp_u, sp_u, 1.0 / m, None, ALU.add)
            tt(sp_u, sp_u, spz, ALU.mult)
            ts(sp_u, sp_u, 1.0, 2.0, ALU.add, ALU.mult)
            tt(sp_u, sp_u, sps, ALU.mult)
            ts(dvf, dvf, 0.0, None, ALU.max)
            tt(dvf, dvf, sp_u, ALU.add)
            tt(dav[:], dtv[:], bc(arow[:], 1, 5), ALU.mult)
            V.tensor_scalar(dav[:], dav[:], -1.0, None, ALU.mult).then_inc(dt_done, 1)

            dv.wait_ge(v_mm, 16)
            for i in range(4, XBC):
                conv(i)
            dv.wait_ge(ds_mm, 1)
            link(V.tensor_copy(dts[:], ps[:, 6, 256:256 + 64].rearrange("p (i b) -> p i b", i=8)))
            tt(eA[:], dts[:], bc(aexp[:], 2, NS), ALU.mult)
            ts(eA[:], eA[:], -1.0, None, ALU.mult)
            dv.wait_ge(silu_done, XBC)
            V.tensor_tensor(xds[:], dts[:], xcX[:, :, NP_:N], ALU.mult).then_inc(ds_ev, 1)

            def sample_c(b):
                dv.wait_ge(hn_done, b + 1)
                tt(smv.rearrange("p (g i) n -> p g i n", g=2), bc(bcb[b][:, 2:4], 2, 4),
                   h0b[b % 2].rearrange("p (g i) n -> p g i n", g=2), ALU.mult)
                V.tensor_reduce(ysm[:, b, :], smv, AX.X, ALU.add).then_inc(smv_done, 1)
                dv.wait_ge(smv_done, b + 1)

            Ug = U[:, 0:G5 * UC].rearrange("p (g c) -> p g c", g=G5)
            dv.wait_ge(lc_mm, 16)
            for c in range(5):
                t0, n = CH[c]
                dv.wait_ge(sa_mm, c + 1)
                link(V.tensor_copy(csv[0:n, 0, :], ps[0:n, 7, 0:16]))
                link(V.tensor_copy(csv[:, 1, :], ps[:, 7, 16:32]))
                link(V.tensor_copy(dev[:, 1, :], csv[:, 1, :]))
                V.tensor_tensor(dev[0:n, 0, :], csv[0:n, 1, :], csv[0:n, 0, :], ALU.subtract).then_inc(de_in, 1)
                tt(cbm[0:n, :, 0:n], ps[0:n, 7, 128:384].rearrange("p (g l) -> p g l", g=2)[:, :, 0:n],
                   bc(tri[0:n, 0:n], 1, 2), ALU.mult)
                for q in range(2):
                    tt(xdt[0:n, 8 * q:8 * q + 8, :], ps[0:n, 4 + q, :].rearrange("p (h d) -> p h d", d=HD),
                       bc(dtv[0:n, c, 8 * q:8 * q + 8], 2, HD), ALU.mult)
                dv.wait_ge(de_out, c + 1)
                V.tensor_tensor(xde[0:n], xdt[0:n], bc(dev[0:n, 0, :], 2, HD), ALU.mult).then_inc(sa_evd, 1)
                if c >= 2:
                    sample_c(2 * c - 4)
                dv.wait_ge(cb_mm, c + 1)
                for h in range(HEADS):
                    last = V.tensor_scalar(Lm[0:n, h, 0:n], ps[0:n, 4 + h // 4, (h % 4) * P:(h % 4) * P + n],
                                           csv[0:n, 0, h:h + 1], 0.0, ALU.subtract, ALU.min)
                    if h % 4 == 3:
                        last.then_inc(l_in, 1)
                if c:
                    dv.wait_ge(e2_done, c + 1)
                    for g in range(2):
                        last = V.tensor_tensor(E2[:, 8 * g:8 * g + 8, 0:n], E2[:, 8 * g:8 * g + 8, 0:n],
                                               bc(xcB[:, 2 + g, t0:t0 + n], 1, 8), ALU.mult)
                    last.then_inc(cs_done, 1)
                dv.wait_ge(l_exp, c + 1)
                for g in range(2):
                    last = V.tensor_tensor(Lm[0:n, 8 * g:8 * g + 8, 0:n], Lm[0:n, 8 * g:8 * g + 8, 0:n],
                                           bc(cbm[0:n, g, 0:n], 1, 8), ALU.mult)
                last.then_inc(m_done, 1)
                if c >= 2:
                    sample_c(2 * c - 3)
                dv.wait_ge(y_mm, c + 1)
                for i in range(8):
                    last = V.scalar_tensor_tensor(ySSD[:, i, t0:t0 + n], xcX[:, i, t0:t0 + n], pf[:, PF_D + i:PF_D + i + 1],
                                                  ps[:, 4 + i // 4, (i % 4) * P:(i % 4) * P + n], ALU.mult, ALU.add)
                last.then_inc(y_ev, 1)
                dv.wait_ge(st_mm, c + 1)
                for g in range(2):
                    hs, pg = Hs[:, 8 * g:8 * g + 8, :], ps[:, 6 + g, :].rearrange("p (h d) -> p h d", d=HD)
                    if c == 0:
                        last = V.tensor_copy(hs, pg)
                    else:
                        tt(hs, hs, bc(dev[:, 1, 8 * g:8 * g + 8], 2, HD), ALU.mult)
                        last = V.tensor_tensor(hs, hs, pg, ALU.add)
                last.then_inc(st_ev, 1)
                if c == 1:
                    for rd in range(16):
                        dv.wait_ge(y5_mm, rd + 1)
                        o = Ug[:, 4 * rd:4 * rd + 4, 0:YC]
                        V.tensor_tensor(o, o, ps[:, 4 + rd % 2, 0:4 * WIN].rearrange("p (q c) -> p q c", q=4)[:, :, 0:YC],
                                        ALU.add).then_inc(y5_ev, 1)
            sample_c(6)
            sample_c(7)
            ys = ySSD[:, :, NP_:N]
            tt(ys, xcX[:, :, NP_:N], bc(pf[:, PF_D:PF_D + 8], 2, NS), ALU.mult)
            tt(ys, ys, ysm[:].rearrange("p b i -> p i b"), ALU.add)
            dv.wait_ge(zs_done, 1)
            dv.wait_ge(y_ev, 5)
            V.tensor_tensor(ySSD, ySSD, zT, ALU.mult).then_inc(gt_done, 1)

            def norm(i, src, gcol):
                dv.wait_ge(ms_done, i + 2)
                root(rmsN, i + 2)
                for k in range(KD):
                    V.scalar_tensor_tensor(src[:, k, :], src[:, k, :], pf[:, gcol + k:gcol + k + 1], rmsN,
                                           ALU.mult, ALU.mult).then_inc(yn_done, 1)

            def low_parts(i, src):
                for k in range(KD):
                    dv.wait_ge(yh_done, 8 * i + k + 1)
                    last = V.tensor_tensor(y_lo[i][:, k, :], src[:, k, :], y_hi[i][:, k, :].bitcast(F32), ALU.subtract)
                last.then_inc(ys_done, 1)

            def sum_squares(i):
                dv.wait_ge(sq_done, KD * (i + 2))
                tt(sq[:, 0:4], sq[:, 0:4], sq[:, 4:8], ALU.add)
                tt(sq[:, 0:2], sq[:, 0:2], sq[:, 2:4], ALU.add)
                V.tensor_tensor(sq[:, 0], sq[:, 0], sq[:, 1], ALU.add).then_inc(sqt_done, 1)

            sum_squares(0)
            for k in range(KD):
                dv.wait_ge(wide_free[k % 2], (28 + k) // 2 + 1)
                V.tensor_tensor(sig[:, k, :], sig[:, k, :], yg[:, k, :], ALU.mult).then_inc(y2_done, 1)
                if k == 3:
                    norm(0, ySSD, PF_GSSD)
                if k == 5:
                    low_parts(0, ySSD)

            def residual_tile(q, i):
                n = TT[i][1]
                o = 5 * q + i
                dv.wait_ge(o_mm, o + 1)
                xs_ = x1[i][0:n, 512 * (q % 2):512 * (q % 2) + 512]
                V.tensor_tensor(xs_, xs_, ps[0:n, o % 4, :], ALU.add).then_inc(o_ev, 1)

            def residual(q):
                for i in range(5):
                    residual_tile(q, i)

            def token_root(i, want):
                s_ = ssum[:, i:i + 1]
                V.tensor_scalar(s_, s_, 1.0 / D, EPS, ALU.mult, ALU.add).then_inc(root_in, 1)
                dv.wait_ge(root_out, want)
                link(V.reciprocal(s_, s_))

            sum_squares(1)
            dv.wait_ge(x1_ld, 80)
            residual(0)
            norm(1, sig, PF_GS5)
            low_parts(1, sig)
            for q in range(1, 3):
                residual(q)

            def moe_norm(i):
                n = TT[i][1]
                dv.wait_ge(xs_sq, i + 1)
                token_root(i, 4 + i)
                if i:
                    dv.wait_ge(x2t_mm, i)
                    dv.wait_ge(x2_st, 16 * i)
                V.scalar_tensor_tensor(x2[0:n, :], x1[i][0:n], ssum[0:n, i:i + 1], gffn[0:n, :],
                                       ALU.mult, ALU.mult).then_inc(x2_done, 1)

            dv.wait_ge(moe_ld, 32)
            for i in range(5):
                residual_tile(3, i)
                moe_norm(i)
            link(V.memset(lgt, 0.0))
            dv.wait_ge(lgt_mm, 5)
            link(V.tensor_copy(lgt[:, 0:4, :], ps[:, 7, 0:144].rearrange("p (i c) -> p i c", i=4)))
            link(V.tensor_copy(lgt[0:24, 4, :], ps[0:24, 7, 144:180]))
            lc = lgt[:, :, 0:EG]
            lf = lgt[:, :, EG:36].rearrange("p i (g e) -> p i g e", g=EG)
            io4, io8 = bc(cst[:, C_IO:C_IO + EG], 1, 5), bc(cst[:, C_IO:C_IO + EPG], 1, 5)

            def first_max(src, m, hot, tmp, iot, w):
                link(V.tensor_reduce(m, src, AX.X, ALU.max))
                tt(tmp, src, bc(m, 2, w), ALU.is_equal)
                ts(tmp, tmp, -99.0, 99.0, ALU.mult, ALU.add)
                tt(tmp, tmp, iot, ALU.add)
                link(V.tensor_reduce(r5, tmp, AX.X, ALU.min))
                tt(hot, iot, bc(r5, 2, w), ALU.is_equal)

            first_max(lc, rm, og, t4, io4, EG)
            V.tensor_tensor(rexp, lc, bc(rm, 2, EG), ALU.subtract).then_inc(r_in, 1)
            t48 = t32.rearrange("p i (g e) -> p i g e", g=EG)
            tt(t48, lf, bc(og, 3, EPG), ALU.mult)
            link(V.tensor_reduce(lsel, t48.rearrange("p i g e -> p i e g"), AX.X, ALU.add))
            first_max(lsel, m1_, o1, t8, io8, EPG)
            stt(lsel, o1, -1e30, lsel, ALU.mult, ALU.add)
            first_max(lsel, m2_, o2, t8, io8, EPG)
            V.tensor_tensor(rdif, m2_, m1_, ALU.subtract).then_inc(r_in, 1)
            val = bc(cst[:, C_VAL:C_VAL + 5], 2, EG)
            tt(og, og, val, ALU.mult)
            for O_, o_ in ((O1, o1), (O2, o2)):
                tt(O_.rearrange("p i (g e) -> p i g e", g=EG), bc(og, 3, EPG), bc(o_, 2, EG), ALU.mult)
            V.tensor_tensor(Ob, O1, O2, ALU.add).then_inc(ob_done, 1)
            link(V.memset(cn[:, 2, 0:1], 0.0))
            dv.wait_ge(rank_mm, 1)
            ts(cn[:, 1, :], ps[:, 7, 256 + 5 * E:256 + 6 * E], 1.0 / T, (T - 1) / (2 * T), ALU.mult, ALU.add)
            ts(cn[:, 1, :], cn[:, 1, :], MAGIC, MAGIC, ALU.add, ALU.subtract)
            ts(cn[:, 1, :], cn[:, 1, :], 1.0, None, ALU.max)
            link(V.tensor_copy(cn[:, 2, 1:E], cn[:, 1, 0:E - 1]))
            src_, dst_ = 2, 0
            sh = 1
            while sh < E:
                link(V.tensor_copy(cn[:, dst_, 0:sh], cn[:, src_, 0:sh]))
                tt(cn[:, dst_, sh:E], cn[:, src_, sh:E], cn[:, src_, 0:E - sh], ALU.add)
                src_, dst_ = dst_, src_
                sh *= 2
            ahead = cn[:, src_, :]
            link(V.tensor_copy(cum[0:1, 0:E], ahead[0:1, :]))
            tt(cum[0:1, E:E + 1], ahead[0:1, E - 1:E], cn[0:1, 1, E - 1:E], ALU.add)
            stt(rank, bc(ahead, 1, 5), float(T), ps[:, 7, 256:256 + 5 * E].rearrange("p (i e) -> p i e", i=5),
                ALU.mult, ALU.add)
            for k, O_ in enumerate((O1, O2)):
                tt(t32, O_, rank, ALU.mult)
                link(V.tensor_reduce(slf[:, :, k], t32, AX.X, ALU.add))
            V.tensor_copy(slot[:], slf).then_inc(slot_done, 1)
            ts(stf, slf, 1.0 / T, (T - 1) / (2 * T), ALU.mult, ALU.subtract)
            ts(stf, stf, MAGIC, MAGIC, ALU.add, ALU.subtract)
            stt(slf, stf, -float(T), slf, ALU.mult, ALU.add)
            flat = lambda v: v.rearrange("p i k -> p (i k)")
            io64 = cst[:, C_IO:C_IO + T]
            tt(oh_row, bc(flat(slf), 2, T), bc(io64, 1, 10), ALU.is_equal)
            tt(oh_tile, bc(flat(stf), 2, IDXC), bc(io64[:, 0:IDXC], 1, 10), ALU.is_equal)
            oh4 = oh_tile.rearrange("p (i k) c -> p i (k c)", k=2)
            V.tensor_tensor(oh4, oh4, bc(cst[:, C_TOK:C_TOK + 5], 2, 2 * IDXC), ALU.mult).then_inc(oh_done, 1)
            dv.wait_ge(r_out, 2)
            link(V.tensor_reduce(rm, rexp, AX.X, ALU.add))
            ts(r5, rdif, 1.0, None, ALU.add)
            tt(rm, rm, r5, ALU.mult)
            link(V.reciprocal(gate[:, 0, :], rm))
            tt(gate[:, 1, :], gate[:, 0, :], rdif, ALU.mult)
            dv.wait_ge(tab_mm, 1)
            V.tensor_copy(idx[:], ps[0:T, 6, 0:IDXC]).then_inc(tab_ev, 1)

            dv.wait_ge(slot_done, 1)
            nt = tile_bound(dv, slice(E, E + 1), E)
            dv.sem_inc(hr, 1)
            dv.wait_ge(xtr, 2)
            V.tensor_copy(xtf, ps[:, 2, :]).then_inc(xev, 1)
            with dv.Fori(0, nt) as q:
                dv.wait_ge(silu, q + 2)
                dv.wait_ge(umm, q + 1)
                dv.wait_ge(htr, q + 1)
                V.tensor_tensor(hh, sg, ps[:, 1, 0:256], ALU.mult).then_inc(hr, 1)
                dv.wait_ge(xtr, q + 3)
                V.tensor_copy(xtf, ps[:, 2, :]).then_inc(xev, 1)
                dv.wait_ge(htr, q + 2)
                dv.wait_ge(dmm, q + 1)
                V.tensor_copy(ht.rearrange("p a b -> p (a b)"), ps[:, 3, 0:256]).then_inc(hev, 1)
            dv.sem_inc(hr, RING - 1)
            def final_norm(i):
                n = TT[i][1]
                dv.wait_ge(xs_sq, 5 + i + 1)
                token_root(i, 9 + i)
                V.scalar_tensor_tensor(x1[i][0:n], x1[i][0:n], ssum[0:n, i:i + 1], gfin[0:n, :],
                                       ALU.mult, ALU.mult).then_inc(fo_done, 1)

            dv.wait_ge(moe_ld, 48)
            for i, (t0, n) in enumerate(TT):
                dv.wait_ge(gy[i], 32)
                xs_ = x1[i][0:n]
                stt(xs_, G[2 * i][0:n], gate[0:n, 0, i:i + 1], xs_, ALU.mult, ALU.add)
                V.scalar_tensor_tensor(xs_, G[2 * i + 1][0:n], gate[0:n, 1, i:i + 1], xs_,
                                       ALU.mult, ALU.add).then_inc(fin_done, 1)
                if i:
                    final_norm(i - 1)
            final_norm(4)


def kernel(**inputs):
    import concourse.bacc as bacc
    from concourse.bass_utils import run_bass_kernel_spmd as run

    x = {k: np.asarray(v) for k, v in inputs.items()}
    f32 = np.float32
    toks = np.concatenate([x["meta_tokens"], x["x_prompt"][0], x["x_sample"][:, 0]], 0)

    def feat(v):
        v = v.reshape(v.shape[0] // P, P, -1)
        return np.ascontiguousarray(v.transpose(1, 0, 2)).reshape(P, -1)

    def tiles(w):
        w = w.reshape(KD, P, w.shape[1] // P, P)
        return np.ascontiguousarray(w.transpose(2, 1, 0, 3)).reshape(w.shape[2], P, KD * P)

    w_in = x["w_in"][0]
    c_z, c_x, c_b, c_dt, c_u = 0, D, 2 * D, D + 1536, D + 1536 + HEADS
    wi = tiles(np.concatenate([w_in[:, c_u:], w_in[:, c_b:c_dt], w_in[:, c_x:c_b], w_in[:, c_z:c_x]], 1))
    t = lambda v: v.T
    pf = np.concatenate([
        feat(x["norm_mix"][0]), feat(t(x["conv_w"][0])), feat(x["conv_b"][0]), feat(np.repeat(x["d_ssd"][0], HD)),
        feat(x["ssd_norm"][0]), feat(x["s5_norm"][0]), feat(x["b_glu"][0]), feat(np.repeat(x["a_log"][0], HD))], 1)
    two = lambda u, v: np.concatenate([u, v], 0)
    are, aim = t(x["s5_a_re"][0]), t(x["s5_a_im"][0])
    s5p = np.concatenate([two(are, are), two(aim, aim), np.broadcast_to(x["s5_log_dt"][0], (P, G5))], 1)
    cr, ci = (x[k][0].transpose(2, 0, 1).reshape(S5, -1) for k in ("s5_c_re", "s5_c_im"))
    br, bi = (x[k][0].transpose(1, 0, 2).reshape(S5, -1) for k in ("s5_b_re", "s5_b_im"))
    s5stk = np.concatenate([two(cr, ci), two(ci, cr), two(br, bi), two(bi, br)], 1)
    s5bt = np.stack([x["s5_b_re"][0], x["s5_b_im"][0]]).transpose(3, 1, 0, 2).reshape(C5, -1)
    dk = np.zeros((4, 32, 16), f32)
    dk[:, :C5] = x["s5_d"][0].reshape(16, 4, C5).transpose(1, 2, 0)
    cst_in = x["state_ssd_conv"][0].reshape(NS, 3, XBC, P).transpose(3, 1, 2, 0).reshape(P, -1)
    h0s5 = np.stack([x["state_s5_re"][0], x["state_s5_im"][0]]).transpose(0, 3, 1, 2)
    wrt = np.concatenate([x["router_coarse_w"][0], x["router_fine_w"][0].transpose(1, 0, 2).reshape(D, E)], 1)
    br_ = np.concatenate([x["router_coarse_b"][0], x["router_fine_b"][0].reshape(-1)])[:, None]
    i = np.arange(P)
    cs = np.zeros((P, C_N), f32)
    cs[:, C_ID:C_ID + P] = np.eye(P)
    cs[:, C_TRI:C_TRI + P] = i[:, None] <= i[None]
    cs[:, C_SGN], cs[:, C_M0], cs[:, C_M1] = np.where(i < 64, 1, -1), i < 64, i >= 64
    tok = i[:, None] + P * np.arange(5)
    cs[:, C_VAL:C_VAL + 5], cs[:, C_TOK:C_TOK + 5] = tok < N, np.where(tok < N, tok, 0)
    cs[:, C_IO:C_IO + T] = np.arange(T)
    onb = np.concatenate([np.ones((P, P)), i[:, None] < i[None]], 1).astype(mybir.dt.np(BF16))

    ins = {
        "consts": cs, "onb": onb, "pf": pf, "xT": feat(t(toks)), "xtok": toks, "wi": wi, "wglu": tiles(x["w_glu"][0]),
        "wdt": feat(w_in[:, c_dt:c_u]), "dtb": x["dt_bias"][0][:, None], "alog": x["a_log"][0],
        "s5p": s5p, "s5stk": s5stk, "s5bt": s5bt, "s5dk": dk.reshape(P, 16), "h0s5": h0s5.reshape(2, S5, NS * G5),
        "cst_in": cst_in, "ssm_in": x["state_ssd_ssm"][0].reshape(NS, HEADS * HD, NSTATE),
        "w_out": x["w_out"][0], "wr": feat(wrt), "br": br_, "gffn": x["norm_ffn"][0], "gfin": x["norm_final"],
        "w_gate": x["w_gate"][0], "w_up": x["w_up"][0], "w_down": x["w_down"][0],
    }
    ins = {k: np.ascontiguousarray(v) for k, v in ins.items()}
    outs = {
        "o_y": (N, D), "o_conv_p": (P, XBC * 3), "o_conv_s": (P, XBC * NS * 3), "o_ssm_p": (P, HEADS * HD),
        "o_ssm_s": (NS, HEADS * HD, NSTATE), "o_s5p": (2, S5, G5), "o_s5s": (2, S5, NS * G5),
    }
    nc = bacc.Bacc("TRN2", target_bir_lowering=False, num_devices=1)
    a = {k: nc.dram_tensor(k, v.shape, mybir.dt.from_np(v.dtype), kind="ExternalInput").ap() for k, v in ins.items()}
    a |= {k: nc.dram_tensor(k, s, F32, kind="ExternalOutput").ap() for k, s in outs.items()}
    build(nc, a)
    r = run(nc, [ins], core_ids=[0]).results[0]
    y = r["o_y"]
    unfeat = lambda v, *s: v.reshape(P, XBC, -1).transpose(2, 1, 0).reshape(*s)
    s5p_o, s5s_o = r["o_s5p"], r["o_s5s"].reshape(2, S5, NS, G5)
    res = (
        y[META:NP_][None], y[NP_:][:, None],
        unfeat(r["o_conv_p"], 1, 1, 3, XBC * P),
        r["o_ssm_p"].T.reshape(1, 1, HEADS, HD, NSTATE),
        s5p_o[0].T[None, None], s5p_o[1].T[None, None],
        r["o_conv_s"].reshape(P, 3, XBC, NS).transpose(3, 1, 2, 0).reshape(1, NS, 3, XBC * P),
        r["o_ssm_s"].reshape(1, NS, HEADS, HD, NSTATE),
        s5s_o[0].transpose(1, 2, 0)[None], s5s_o[1].transpose(1, 2, 0)[None],
    )
    return tuple(np.ascontiguousarray(v) for v in res)
```
